# Optimizing a Trainium2 kernel written in Bass

```python
import jax, jax.numpy as jnp
from jax import lax
import numpy as np

D_MODEL = 1024
BATCH = 1
SEQ = 256
DEPTH = 2
DEC_BATCH = 8
DEC_SEQ = 1
PAST_LEN = 2048
PAGE_SIZE = 128

D_A = D_MODEL // 2
H_A = 4
DK_A = D_A // H_A
DV_A = D_A // H_A
D_B = D_MODEL // 2
NB_B = 4
BS_B = D_B // NB_B
CONV_W = 4
RG_C = 8.0
H_C = 4
D_C = D_MODEL // 2
DK_C_TOT = D_MODEL // 4
DK_C = DK_C_TOT // H_C
DV_C = D_C // H_C
GATE_RANK = 16
GLA_TAU = 16.0
CHUNK = 64
FFN_DIM = 2816
N_SUB = 3
EPS = 1e-6
IN_SPLITS = (D_A, D_A, D_A, D_A, D_B, D_B, DK_C_TOT, DK_C_TOT, D_C, D_C, GATE_RANK, D_MODEL, D_MODEL, D_MODEL)
N_IN = sum(IN_SPLITS)

kernel_name = 'hybrid_hgrn2_rglru_gla_macaron_adaln_step'

def rmsnorm(x, g):
    xf = x.astype(jnp.float32)
    y = xf * lax.rsqrt(jnp.mean(xf * xf, axis=-1, keepdims=True) + EPS)
    return (y * g.astype(jnp.float32)).astype(x.dtype)

def ada_norm(x, g, shift, scale):
    return rmsnorm(x, g) * (1 + scale) + shift

def swiglu(h, w_i, w_o):
    gt, up = jnp.split(h @ w_i, 2, axis=-1)
    return (jax.nn.silu(gt) * up) @ w_o

def chunked_gated_recurrence(q, k, v, log_f, s0):
    B, T, H, DK = q.shape
    DV = v.shape[-1]
    C = min(CHUNK, T)
    n = -(-T // C)
    pad = n * C - T
    f32 = jnp.float32

    def to_chunks(a):
        a = a.astype(f32)
        if pad:
            a = jnp.pad(a, ((0, 0), (0, pad), (0, 0), (0, 0)))
        return a.reshape(B, n, C, H, a.shape[-1]).transpose(1, 0, 3, 2, 4)

    qc, kc, vc, gc = to_chunks(q), to_chunks(k), to_chunks(v), to_chunks(log_f)
    causal = jnp.tril(jnp.ones((C, C), dtype=bool))[:, :, None]

    def step(S, inp):
        qb, kb, vb, gb = inp
        b = jnp.cumsum(gb, axis=2)
        inter = jnp.einsum('bhtd,bhdv->bhtv', qb * jnp.exp(b), S)
        diff = b[:, :, :, None, :] - b[:, :, None, :, :]
        decay = jnp.exp(jnp.where(causal, diff, -jnp.inf))
        scores = jnp.einsum('bhtd,bhsd,bhtsd->bhts', qb, kb, decay)
        intra = jnp.einsum('bhts,bhsv->bhtv', scores, vb)
        b_end = b[:, :, -1:, :]
        S_new = jnp.exp(b_end[:, :, 0, :])[..., None] * S + jnp.einsum(
            'bhsd,bhsv->bhdv', kb * jnp.exp(b_end - b), vb)
        return S_new, inter + intra

    S_fin, o = lax.scan(step, s0.astype(f32), (qc, kc, vc, gc))
    o = o.transpose(1, 0, 3, 2, 4).reshape(B, n * C, H, DV)[:, :T]
    return o.astype(v.dtype), S_fin.astype(s0.dtype)

def head_out(o, gain, g):
    B, T, H, DV = o.shape
    return rmsnorm(o, gain).reshape(B, T, H * DV) * jax.nn.silu(g)

def rglru_branch(xb, gb, buf, h0, conv_w, conv_b, wa, ba, wx, bx, lam):
    B, T, _ = xb.shape
    f32 = jnp.float32
    xpad = jnp.concatenate([buf.astype(xb.dtype), xb], axis=1)
    conv = conv_b
    for j in range(CONV_W):
        conv = conv + xpad[:, j:j + T] * conv_w[j]
    new_buf = xpad[:, T:]
    xr = conv.reshape(B, T, NB_B, BS_B)
    r = jax.nn.sigmoid((jnp.einsum('btnk,nkj->btnj', xr, wa).reshape(B, T, D_B) + ba).astype(f32))
    i = jax.nn.sigmoid((jnp.einsum('btnk,nkj->btnj', xr, wx).reshape(B, T, D_B) + bx).astype(f32))
    log_a = -RG_C * r * jax.nn.softplus(-lam.astype(f32))
    a = jnp.exp(log_a)
    u = jnp.sqrt(-jnp.expm1(2.0 * log_a)) * i * conv.astype(f32)

    def combine(lft, rgt):
        a1, b1 = lft
        a2, b2 = rgt
        return a1 * a2, a2 * b1 + b2

    a_cum, u_cum = lax.associative_scan(combine, (a, u), axis=1)
    h = u_cum + a_cum * h0.astype(f32)[:, None]
    y = jax.nn.gelu(gb) * h.astype(gb.dtype)
    return y, new_buf, h[:, -1].astype(h0.dtype)

def mixer_block(h, lb, st_a, st_cv, st_h, st_c, w_in, hgrn_norm, conv_w, conv_b, rg_wa, rg_ba,
                rg_wx, rg_bx, rg_lam, gla_wa, gla_ba, gla_norm, w_br_a, w_br_b, w_br_c, w_out):
    B, T, _ = h.shape
    f32 = jnp.float32
    idx = np.cumsum(IN_SPLITS)[:-1].tolist()
    (a_q, a_f, a_i, a_g, b_x, b_g, c_q, c_k, c_v, c_g, c_a,
     m_a, m_b, m_c) = jnp.split(h @ w_in, idx, axis=-1)

    fz = a_f.astype(f32)
    log_f_a = jnp.logaddexp(jnp.log(lb), jnp.log1p(-lb) + jax.nn.log_sigmoid(fz))
    k_a = (1 - lb) * jax.nn.sigmoid(-fz)
    o_a, s_a = chunked_gated_recurrence(
        jax.nn.silu(a_q).reshape(B, T, H_A, DK_A), k_a.reshape(B, T, H_A, DK_A),
        a_i.reshape(B, T, H_A, DV_A), log_f_a.reshape(B, T, H_A, DK_A), st_a)
    y_a = head_out(o_a, hgrn_norm, a_g)

    y_b, new_cv, new_h = rglru_branch(b_x, b_g, st_cv, st_h, conv_w, conv_b,
                                      rg_wa, rg_ba, rg_wx, rg_bx, rg_lam)

    log_f_c = jax.nn.log_sigmoid((c_a @ gla_wa + gla_ba).astype(f32)) / GLA_TAU
    o_c, s_c = chunked_gated_recurrence(
        c_q.reshape(B, T, H_C, DK_C) * (DK_C ** -0.5), c_k.reshape(B, T, H_C, DK_C),
        c_v.reshape(B, T, H_C, DV_C), log_f_c.reshape(B, T, H_C, DK_C), st_c)
    y_c = head_out(o_c, gla_norm, c_g)

    merged = (jax.nn.sigmoid(m_a) * (y_a @ w_br_a) + jax.nn.sigmoid(m_b) * (y_b @ w_br_b)
              + jax.nn.sigmoid(m_c) * (y_c @ w_br_c))
    return merged @ w_out, s_a, new_cv, new_h, s_c

def setup_inputs(seed: int = 0) -> dict:
    key = jax.random.key(seed)
    ks = iter(jax.random.split(key, 40))
    nrm = lambda shape, s: s * jax.random.normal(next(ks), shape, jnp.float32)
    a0 = jax.random.uniform(next(ks), (DEPTH, D_B), jnp.float32, minval=0.9, maxval=0.999)
    return {
        'x_prompt': nrm((BATCH, SEQ, D_MODEL), 1.0),
        'x_sample': nrm((DEC_BATCH, DEC_SEQ, D_MODEL), 1.0),
        'c_prompt': nrm((BATCH, D_MODEL), 1.0),
        'c_sample': nrm((DEC_BATCH, D_MODEL), 1.0),
        'state_hgrn': nrm((DEPTH, DEC_BATCH, H_A, DK_A, DV_A), 1.0),
        'state_conv': nrm((DEPTH, DEC_BATCH, CONV_W - 1, D_B), 1.0),
        'state_rglru': nrm((DEPTH, DEC_BATCH, D_B), 0.5),
        'state_gla': nrm((DEPTH, DEC_BATCH, H_C, DK_C, DV_C), 1.0),
        'w_ada': nrm((DEPTH, D_MODEL, N_SUB * 3 * D_MODEL), D_MODEL ** -0.5),
        'b_ada': nrm((DEPTH, N_SUB * 3 * D_MODEL), 0.02),
        'norm_gain': 1.0 + nrm((DEPTH, N_SUB, D_MODEL), 0.02),
        'w_ffn_in': nrm((DEPTH, 2, D_MODEL, 2 * FFN_DIM), D_MODEL ** -0.5),
        'w_ffn_out': nrm((DEPTH, 2, FFN_DIM, D_MODEL), FFN_DIM ** -0.5),
        'w_in': nrm((DEPTH, D_MODEL, N_IN), D_MODEL ** -0.5),
        'hgrn_lb_logits': nrm((DEPTH, D_A), 0.1),
        'hgrn_norm': 1.0 + nrm((DEPTH, DV_A), 0.02),
        'conv_w': nrm((DEPTH, CONV_W, D_B), CONV_W ** -0.5),
        'conv_b': nrm((DEPTH, D_B), 0.02),
        'rg_wa': nrm((DEPTH, NB_B, BS_B, BS_B), BS_B ** -0.5),
        'rg_ba': nrm((DEPTH, D_B), 0.02),
        'rg_wx': nrm((DEPTH, NB_B, BS_B, BS_B), BS_B ** -0.5),
        'rg_bx': nrm((DEPTH, D_B), 0.02),
        'rg_lambda': jnp.log(a0) - jnp.log1p(-a0),
        'gla_w_alpha': nrm((DEPTH, GATE_RANK, DK_C_TOT), GATE_RANK ** -0.5),
        'gla_b_alpha': nrm((DEPTH, DK_C_TOT), 0.02),
        'gla_norm': 1.0 + nrm((DEPTH, DV_C), 0.02),
        'w_br_a': nrm((DEPTH, D_A, D_MODEL), D_A ** -0.5),
        'w_br_b': nrm((DEPTH, D_B, D_MODEL), D_B ** -0.5),
        'w_br_c': nrm((DEPTH, D_C, D_MODEL), D_C ** -0.5),
        'w_out': nrm((DEPTH, D_MODEL, D_MODEL), D_MODEL ** -0.5),
        'final_norm': 1.0 + nrm((D_MODEL,), 0.02),
    }

def reference(x_prompt, x_sample, c_prompt, c_sample, state_hgrn, state_conv, state_rglru, state_gla,
              w_ada, b_ada, norm_gain, w_ffn_in, w_ffn_out, w_in, hgrn_lb_logits, hgrn_norm,
              conv_w, conv_b, rg_wa, rg_ba, rg_wx, rg_bx, rg_lambda, gla_w_alpha, gla_b_alpha,
              gla_norm, w_br_a, w_br_b, w_br_c, w_out, final_norm):
    lb_all = jnp.cumsum(jax.nn.softmax(hgrn_lb_logits.astype(jnp.float32), axis=0), axis=0)
    lb_all = lb_all - lb_all[0]

    def run(x, c, s_a, s_cv, s_h, s_c):
        B = x.shape[0]
        na, ncv, nh, nc = [], [], [], []
        for l in range(DEPTH):
            mod = (c @ w_ada[l] + b_ada[l]).reshape(B, N_SUB, 3, D_MODEL)[:, :, :, None, :]
            h = ada_norm(x, norm_gain[l, 0], mod[:, 0, 0], mod[:, 0, 1])
            x = x + 0.5 * mod[:, 0, 2] * swiglu(h, w_ffn_in[l, 0], w_ffn_out[l, 0])
            h = ada_norm(x, norm_gain[l, 1], mod[:, 1, 0], mod[:, 1, 1])
            y, sa, scv, sh, sc = mixer_block(
                h, lb_all[l], s_a[l], s_cv[l], s_h[l], s_c[l], w_in[l], hgrn_norm[l],
                conv_w[l], conv_b[l], rg_wa[l], rg_ba[l], rg_wx[l], rg_bx[l], rg_lambda[l],
                gla_w_alpha[l], gla_b_alpha[l], gla_norm[l], w_br_a[l], w_br_b[l], w_br_c[l], w_out[l])
            x = x + mod[:, 1, 2] * y
            h = ada_norm(x, norm_gain[l, 2], mod[:, 2, 0], mod[:, 2, 1])
            x = x + 0.5 * mod[:, 2, 2] * swiglu(h, w_ffn_in[l, 1], w_ffn_out[l, 1])
            na.append(sa); ncv.append(scv); nh.append(sh); nc.append(sc)
        return (rmsnorm(x, final_norm), jnp.stack(na), jnp.stack(ncv), jnp.stack(nh), jnp.stack(nc))

    Bp = x_prompt.shape[0]
    dt = x_prompt.dtype
    y_prompt, hgrn_p, conv_p, rglru_p, gla_p = run(
        x_prompt, c_prompt,
        jnp.zeros((DEPTH, Bp, H_A, DK_A, DV_A), dt),
        jnp.zeros((DEPTH, Bp, CONV_W - 1, D_B), dt),
        jnp.zeros((DEPTH, Bp, D_B), dt),
        jnp.zeros((DEPTH, Bp, H_C, DK_C, DV_C), dt))
    y_sample, hgrn_s, conv_s, rglru_s, gla_s = run(
        x_sample, c_sample, state_hgrn, state_conv, state_rglru, state_gla)
    return (y_prompt, y_sample, hgrn_p, hgrn_s, conv_p, conv_s, rglru_p, rglru_s, gla_p, gla_s)


_drawn_inputs = setup_inputs


def setup_inputs(seed=0):
    import zlib

    import numpy as np

    out = dict(_drawn_inputs(seed))
    spreads = {}
    factors = {'hgrn_norm': 4.955,
     'conv_b': 2.745,
     'rg_ba': 8.0,
     'rg_bx': 7.784,
     'gla_b_alpha': 4.283,
     'gla_norm': 5.151,
     'final_norm': 2.765}
    for name, (base, spread) in spreads.items():
        noise = np.random.default_rng([zlib.crc32(name.encode()), seed]).standard_normal(out[name].shape)
        drawn = base * np.exp(spread * noise) if base else spread * noise
        out[name] = __import__('jax').numpy.asarray(drawn.astype(out[name].dtype))
    for name, factor in factors.items():
        out[name] = (out[name] * factor).astype(out[name].dtype)
    return out
```

```python
import concourse.bass as bass
from concourse import mybir
from contextlib import ExitStack

F = mybir.dt.float32
FR = mybir.dt.float32r
I32 = mybir.dt.int32
ACT = mybir.ActivationFunctionType
ALU = mybir.AluOpType

P = 128
D = 1024
KT = D // P
T, NB = 256, 8
NT = T + NB
NL = 2
FFN = 2816
FT = FFN // P
H = 4
EPS = 1e-6
SLOTS, UC = 4, 1024
ADA_C = 512
NADA = 3 * D // ADA_C

U_ADA, U_IN, U_OUT, U_MIX = 4 * NADA, 2 * FT, 3 * KT, 84
BASE = {}
_at = 0
for _name, _n in (("ada0", U_ADA), ("in0", U_IN), ("out0", U_OUT), ("ada1", U_ADA), ("mix", U_MIX),
                  ("ada2", U_ADA), ("in1", U_IN), ("out1", U_OUT)):
    BASE[_name] = _at
    _at += _n
UNITS = _at
LOOK = 3

C_AQ, C_AF, C_AI, C_AG, C_BX, C_BG = 0, 512, 1024, 1536, 2048, 2560
C_CQ, C_CK, C_CV, C_CG, C_CA, C_MA, C_MB, C_MC = 3072, 3328, 3584, 4096, 4608, 4624, 5648, 6672


def mixer_units():
    out = []
    for kind, n in (("f", 4), ("q", 4), ("i", 4)):
        out += [("in", kind, j) for j in range(n)]
    out += [("ca", "ca", 0), ("ca", "ca", 1)]
    for kind, n in (("cq", 2), ("ck", 2), ("cv", 4), ("bx", 4), ("bg", 4)):
        out += [("in", kind, j) for j in range(n)]
    out += [("rg", "wa", 0), ("rg", "wx", 0)]
    for kind, n in (("cg", 4), ("ag", 4), ("ma", 8)):
        out += [("in", kind, j) for j in range(n)]
    for j in range(4):
        out += [("in", "mb", 2 * j), ("in", "mb", 2 * j + 1), ("br", "b", j)]
    out += [("br", "a", j) for j in range(4)]
    for j in range(4):
        out += [("in", "mc", 2 * j), ("in", "mc", 2 * j + 1), ("br", "c", j)]
    out += [("out", "o", j) for j in range(8)]
    return out


MIX = mixer_units()
assert len(MIX) == U_MIX
COLS = dict(f=C_AF, q=C_AQ, i=C_AI, cq=C_CQ, ck=C_CK, cv=C_CV, bx=C_BX, bg=C_BG, cg=C_CG, ag=C_AG,
            ma=C_MA, mb=C_MB, mc=C_MC)
BY_ACT = {"f", "q", "bx", "bg", "wa", "wx", "cg", "ag", "ma", "mb", "mc"}


def mixer_groups():
    out = []
    for u, (kind, what, j) in enumerate(MIX):
        e = "A" if what in BY_ACT else "V"
        if kind in ("in", "out"):
            out.append((e, what, j, u))
        elif kind == "ca" and j == 1:
            out.append((e, what, 0, u))
        elif kind == "rg":
            out += [(e, what, n, u) for n in range(4)]
        elif kind == "br":
            out += [(e, "br" + what, 2 * j + n, u) for n in range(2)]
    return out


MG = mixer_groups()
GI = {(what, j): n for n, (_, what, j, _) in enumerate(MG)}
EV_IN, EV_OUT, EV_MIX = "AV" * FT, "V" * KT, "".join(g[0] for g in MG)
EV = EV_IN + EV_OUT + EV_MIX + EV_IN + EV_OUT
G_BASE = {"in0": 0, "out0": 2 * FT, "mix": 2 * FT + KT, "in1": 2 * FT + KT + len(MG),
          "out1": 4 * FT + KT + len(MG)}
EV_TOT = {e: EV.count(e) for e in "AV"}


def ev_count(e, g):
    return EV[:g].count(e)


SCRATCH = 4096
PC = dict(gain=0, convw=24, convb=40, rba=44, rbx=48, lam=52, glab=56, hnorm=58, gnorm=59, lb=60,
          fnorm=68, bada=76, L1=148, l1m=152, oml=156, nsp=160)
NPAR = 164

LEVELS = [0, 1, 2, 4, 8, 16, 32, 64, 128]

PE_LV = {"A": [16 + 4 * i for i in range(9)], "C": [25 + 3 * i for i in range(9)]}
BATCHES = [("A", 0), ("A", 1), ("A", 2), ("A", 3), ("C", 0), ("C", 1)]


def trunk(nc, x_prompt, x_sample, c_prompt, c_sample, state_hgrn, state_conv, state_rglru, state_gla,
          w_ada, b_ada, norm_gain, w_ffn_in, w_ffn_out, w_in, hgrn_lb_logits, hgrn_norm, conv_w,
          conv_b, rg_wa, rg_ba, rg_wx, rg_bx, rg_lambda, gla_w_alpha, gla_b_alpha, gla_norm, w_br_a,
          w_br_b, w_br_c, w_out, final_norm, y_p, y_s, hg_p, hg_s, cv_p, cv_s, rl_p, rl_s, gl_p, gl_s):
    ctx = ExitStack()
    with ctx:
        def sem(name):
            return ctx.enter_context(nc.semaphore(name))

        def sb(name, shape, dt=F, c=ctx):
            return c.enter_context(nc.sbuf_tensor(name, shape, dt))

        raw = sb("raw", [P, SLOTS, UC])
        whi = sb("whi", [P, SLOTS, UC], FR)
        wlo = sb("wlo", [P, SLOTS, UC], FR)
        x = sb("x", [P, KT, NT])
        hH = sb("hH", [P, KT, NT], FR)
        hL = sb("hL", [P, KT, NT], FR)
        tmp = sb("tmp", [P, KT, NT])
        mod = sb("mod", [P, 72, 9])
        Gs = sb("Gs", [P, KT, 9])
        gate = sb("gate", [P, KT, 9])
        par_all = sb("par_all", [P, NL, NPAR])
        par = sb("par", [P, NPAR])
        cst = sb("cst", [P, KT, P], FR)
        ident = sb("ident", [P, P])
        ones = sb("ones", [P, T])
        sel = sb("sel", [64, 9])
        mask = sb("mask", [P, 8, P])
        ada_row = sb("ada_row", [64, 2, ADA_C])
        rstd = sb("rstd", [P, 1, NT])
        t8 = sb("t8", [P, KT, NB])
        epst = sb("epst", [P, 1])
        sc = {"A": sb("scA", [P, H, 384]), "C": sb("scC", [P, H, 384])}
        VTA = sb("VTA", [P, 2, 512])
        st = sb("st", [P, 2, NB, P])
        vblk1 = sb("vblk1", [40, NB * P])
        sTs = sb("sTs", [40, 2, 512])
        wal = sb("wal", [16, 256])
        tail = sb("tail", [P, 4, 20])
        cbuf = sb("cbuf", [P, 4, 32])
        fS = sb("fS", [P, 6, NB])
        with ExitStack() as c0:
            stage = sb("stage", [P, 2, D], c=c0)
            xc = sb("xc", [16, 2, D], c=c0)
            rows = sb("rows", [P, 4, P], c=c0)
            setup_t = sb("setup_t", [P, 8, 16], c=c0)
        with ExitStack() as c1:
            hidH = sb("hidH", [P, FT, NT], FR, c=c1)
            hidL = sb("hidL", [P, FT, NT], FR, c=c1)
            sil = sb("sil", [P, 2, NT], c=c1)
            hid = sb("hid", [P, 2, NT], c=c1)
        c2 = ctx.enter_context(ExitStack())
        yH = sb("yH", [P, 12, NT], FR, c=c2)
        yL = sb("yL", [P, 12, NT], FR, c=c2)
        B = {"A": sb("bA", [P, 4, NT], c=c2), "C": sb("bC", [P, 2, NT], c=c2)}
        Q = {"A": sb("qA", [P, 4, NT], c=c2), "C": sb("qC", [P, 2, NT], c=c2)}
        K = {"A": sb("kA", [P, 4, NT], c=c2), "C": sb("kC", [P, 2, NT], c=c2)}
        V = {"A": sb("vA", [P, 4, NT], c=c2), "C": sb("vC", [P, 4, NT], c=c2)}
        GT = {"A": sb("gA", [P, 4, NT], c=c2), "C": sb("gC", [P, 4, NT], c=c2)}
        ca = sb("ca", [16, NT], c=c2)
        XB = sb("XB", [P, 8, NT], c=c2)
        X = {"A": sb("xA", [P, 2, 4, NT], c=c2), "C": sb("xC", [P, 2, 2, NT], c=c2)}
        sg = sb("sg", [P, 2, NT], c=c2)
        flat = lambda t_: t_[:, :, :].rearrange("p k t -> p (k t)")
        O = {"A": Q["A"], "C": V["C"]}
        VT = {"A": VTA, "C": flat(V["A"])[:, 0:D].rearrange("p (t n) -> p t n", t=2)}
        KTT = flat(K["A"])[:, 0:D].rearrange("p (t n) -> p t n", t=2)
        vblk = [flat(B["A"])[:, 0:D], vblk1[:, :]]
        stF = flat(B["C"])[:, 0:H * P].rearrange("p (h v) -> p h v", h=H)
        crow, hrow = X["A"][0:24, 0, 0:2].rearrange("p k t -> p (k t)"), X["A"][0:NB, 1, 0:2].rearrange("p k t -> p (k t)")
        BK = [ctx.enter_context(nc.psum_tensor(f"bank{i}", [P, 512], F)) for i in range(8)]
        AUX = BK[4:]

        landed = [sem(f"landed{i}") for i in range(SLOTS)]
        hi_done = sem("hi_done")
        lo_done = sem("lo_done")
        unit_done = sem("unit_done")
        evac = {"A": sem("evac_act"), "V": sem("evac_dve")}
        PER = {}
        S = {}

        def event(name, per=1):
            S[name], PER[name] = sem(name), per

        for name, per in (
                ("layer_par", 1), ("ada_ps", 3 * NADA), ("ada_row", 3 * NADA), ("ada_feat", 3 * NADA),
                ("mod_ready", 3 * NADA), ("sq_ready", 3), ("ms_done", 3), ("root_done", 3),
                ("xn_ready", 3), ("G_ready", 3), ("h_p", 3), ("h_s", 3), ("h_hi", 3), ("h_lo", 3),
                ("hid_hi", 2 * FT), ("hid_lo", 2 * FT), ("x_ready", 3),
                ("state_rows", 1), ("rowsT", 1), ("rows_evac", 1),
                ("A_abs", 1), ("C_abs", 1), ("C_logf", 1), ("A_kearg", 1), ("C_kearg", 1), ("A_keexp", 1), ("C_keexp", 1), ("rg_u", 1), ("A_ln", 1), ("A_ls", 1), ("A_k", 1), ("A_diff", 1),
                ("A_ln2", 1), ("A_logf", 1), ("A_cum", 1), ("A_fS", 1), ("C_fS", 1), ("A_kend", 1), ("C_kend", 1),
                ("A_kk", 1), ("C_alpha", 1), ("C_z", 1), ("C_ln", 1), ("C_cum", 1),
                ("A_arg", 8), ("A_exp", 8), ("A_mul", 8), ("A_mm", 9), ("A_sc", 9),
                ("C_arg", 8), ("C_exp", 8), ("C_mul", 8), ("C_mm", 9), ("C_sc", 9),
                ("A_vT", 1), ("A_vTe", 1), ("C_vT", 1), ("C_vTe", 1),
                ("sT", 4), ("sTe", 4),
                ("conv", 1), ("conv_hi", 1), ("conv_lo", 1), ("rg_arg", 1), ("rg_tanh", 1), ("rg_nt", 1),
                ("rg_sqrt", 1), ("yb", 1), ("yb_hi", 1), ("yb_lo", 1), ("tailT", 1), ("tail_evac", 1), ("xb_free", 1),
                ("A_o", 1), ("A_oe", 1), ("C_o", 1), ("C_oe", 1),
                ("A_kT", 1), ("A_kTe", 1), ("C_kT", 1), ("C_kTe", 1),
                ("A_S", 1), ("A_Se", 1), ("C_S", 1), ("C_Se", 1),
                ("vblk", 8), ("st_scaled", 6), ("kv", 6), ("st_new", 6), ("so", 6), ("A_soe", 1), ("C_soe", 1),
                ("A_sq", 1), ("A_ms", 1), ("A_root", 1), ("A_y", 1), ("A_hi", 1), ("A_lo", 1),
                ("C_sq", 1), ("C_ms", 1), ("C_root", 1), ("C_y", 1), ("C_hi", 1), ("C_lo", 1),
                ("mrg", 8), ("m_hi", 8), ("m_lo", 8)):
            event(name, per)
        st_in = [sem(f"st_in{i}") for i in range(2)]
        st_out = [sem(f"st_out{i}") for i in range(2)]
        fin_out = sem("fin_out")
        stored = sem("stored")
        direct = sem("direct")
        rows_in = sem("rows_in")
        wal_in = sem("wal_in")
        dve_set = sem("dve_set")
        dve_seq = sem("dve_seq")
        act_seq = sem("act_seq")
        set_load = [sem(f"set_load{i}") for i in range(3)]
        set_pool, set_pe, set_dve, set_act = (sem(n) for n in ("set_pool", "set_pe", "set_dve", "set_act"))
        fin_dve, fin_act, fin_pe, y_out = (sem(n) for n in ("fin_dve", "fin_act", "fin_pe", "y_out"))
        CREDIT = {"x_ready": 1, "ada_feat": 1}
        settled = sem("settled")
        SEQ = 512

        def wait(eng, name, L, i=0):
            eng.wait_ge(S[name], L * PER[name] + (i + (1 + CREDIT.get(name, 0))))

        def settle(eng):
            eng.sem_inc(settled, 1)

        def unit_no(L, q, s):
            return L * UNITS + q * SLOTS + s

        def bc(ap, shape):
            return ap.broadcast_to(shape)

        def load(sp, L, q, s, dst_shape, src):
            sp.wait_ge(lo_done, unit_no(L, q, s) + 1)
            settle(sp)
            sp.dma_start(dst_shape, src).then_inc(landed[s], 16)

        def split_hi(act, L, q, s, n=UC):
            act.wait_ge(landed[s], (L * (UNITS // SLOTS) + q + 1) * 16)
            act.wait_ge(unit_done, unit_no(L, q, s) + 1)
            nc.scalar.activation(whi[:, s, 0:n], raw[:, s, 0:n], ACT.Copy).then_inc(hi_done, 1)

        def split_lo(dve, L, q, s, n=UC):
            dve.wait_ge(hi_done, unit_no(L, q, s) + 1)
            nc.vector.tensor_tensor(wlo[:, s, 0:n], raw[:, s, 0:n], whi[:, s, 0:n].bitcast(F),
                                    ALU.subtract).then_inc(lo_done, 1)

        def unit_ready(pe, L, q, s):
            pe.wait_ge(lo_done, unit_no(L, q, s) + 1 + SLOTS)

        def unit_used(eng, L, q, s):
            eng.wait_ge(unit_done, unit_no(L, q, s) + 1 + SLOTS)

        def mm3(out, s, col, rh, rl, start, stop):
            a, b = whi[:, s, col:col + P], wlo[:, s, col:col + P]
            nc.tensor.matmul(out, a, rh, start=start, stop=False)
            nc.tensor.matmul(out, a, rl, start=False, stop=False)
            return nc.tensor.matmul(out, b, rh, start=False, stop=stop)

        def bank_free(pe, L, phase, g):
            b = G_BASE[phase]
            if g == 0:
                for e in "AV":
                    pe.wait_ge(evac[e], L * EV_TOT[e] + (ev_count(e, b) + 1))
            elif g >= 4:
                e = EV[b + g - 4]
                pe.wait_ge(evac[e], L * EV_TOT[e] + (ev_count(e, b + g - 3) + 1))

        def mix_qs(u):
            return BASE["mix"] // SLOTS + u // SLOTS, u % SLOTS

        def mix_cols(u):
            return {"in": UC, "ca": 512, "rg": 512, "br": UC, "out": UC}[MIX[u][0]]

        def evacuated(eng, L, what, j):
            g = GI[(what, j)]
            e = MG[g][0]
            eng.wait_ge(evac[e], L * EV_TOT[e] + (ev_count(e, G_BASE["mix"] + g + 1) + 1))

        def mix_hi(act, L, u):
            split_hi(act, L, *mix_qs(u), mix_cols(u))

        def mix_lo(dve, L, u):
            split_lo(dve, L, *mix_qs(u), mix_cols(u))

        OUT_K = (8, 8, 6)

        row_src = []
        for l in range(NL):
            row_src.append([
                (PC["gain"], norm_gain[l].rearrange("s (k p) -> (s k) p", p=P)),
                (PC["convw"], conv_w[l].rearrange("j (k p) -> (j k) p", p=P)),
                (PC["convb"], conv_b[l].rearrange("(k p) -> k p", p=P)),
                (PC["rba"], rg_ba[l].rearrange("(k p) -> k p", p=P)),
                (PC["rbx"], rg_bx[l].rearrange("(k p) -> k p", p=P)),
                (PC["lam"], rg_lambda[l].rearrange("(k p) -> k p", p=P)),
                (PC["glab"], gla_b_alpha[l].rearrange("(k p) -> k p", p=P)),
                (PC["hnorm"], hgrn_norm[l:l + 1, :]),
                (PC["gnorm"], gla_norm[l:l + 1, :]),
                (PC["lb"], hgrn_lb_logits.rearrange("l (k p) -> (l k) p", p=P)),
                (PC["fnorm"], final_norm.rearrange("(k p) -> k p", p=P)),
            ])
        N_ROWS = sum(len(r) for r in row_src) + NL

        block = ctx.enter_context(nc.Block())

        @block.sync
        def _(sp):
            r3 = lambda ap, k: ap.rearrange("p (k n) -> p k n", k=k)

            def ada(L, sub):
                with sp.Fori(0, NADA) as c:
                    for s in range(SLOTS):
                        src = w_ada[bass.ds(L, 1), s * 256:(s + 1) * 256, bass.ds(c * ADA_C + sub * 3 * D, ADA_C)]
                        load(sp, L, BASE[f"ada{sub}"] // SLOTS + c, s, r3(raw[:, s], 2),
                             src.rearrange("o (k p) n -> p (o k) n", p=P))

            def ffn(L, f):
                with sp.Fori(0, FT // 2) as i:
                    for s in range(SLOTS):
                        col = (i * 2 + s // 2) * P + (s % 2) * FFN
                        src = w_ffn_in[bass.ds(L, 1), f, :, bass.ds(col, P)]
                        load(sp, L, BASE[f"in{f}"] // SLOTS + i, s, r3(raw[:, s], KT),
                             src.rearrange("o (k p) n -> p (o k) n", p=P))
                with sp.Fori(0, 2) as i:
                    for u in range(12):
                        t, part = u // 3, u % 3
                        src = w_ffn_out[bass.ds(L, 1), f, part * 8 * P:(part * 8 + OUT_K[part]) * P,
                                        bass.ds((i * 4 + t) * P, P)]
                        load(sp, L, BASE[f"out{f}"] // SLOTS + i * 3 + u // SLOTS, u % SLOTS,
                             r3(raw[:, u % SLOTS, 0:OUT_K[part] * P], OUT_K[part]),
                             src.rearrange("o (k p) n -> p (o k) n", p=P))

            def mixer(L):
                for u, (kind, what, j) in enumerate(MIX):
                    q, s = mix_qs(u)
                    lx = bass.ds(L, 1)
                    if kind == "in":
                        c = COLS[what] + j * P
                        dst, src = r3(raw[:, s], KT), w_in[lx, :, c:c + P]
                    elif kind == "ca":
                        dst, src = r3(raw[:, s, 0:512], 4), w_in[lx, j * 512:(j + 1) * 512, C_CA:C_CA + P]
                    elif kind == "rg":
                        w = rg_wa if what == "wa" else rg_wx
                        load(sp, L, q, s, r3(raw[:, s, 0:512], 4), w[lx].rearrange("o n k j -> k (o n) j"))
                        continue
                    elif kind == "br":
                        w = {"a": w_br_a, "b": w_br_b, "c": w_br_c}[what]
                        dst, src = r3(raw[:, s], 4), w[lx, :, j * 256:(j + 1) * 256]
                    else:
                        dst, src = r3(raw[:, s], KT), w_out[lx, :, j * P:(j + 1) * P]
                    load(sp, L, q, s, dst, src.rearrange("o (k p) n -> p (o k) n", p=P))

            with sp.Fori(0, NL) as L:
                ada(L, 0)
                ffn(L, 0)
                ada(L, 1)
                mixer(L)
                ada(L, 2)
                ffn(L, 1)
            for s in range(SLOTS):
                sp.wait_ge(landed[s], NL * UNITS // SLOTS * 16)

        @block.tensor
        def _(pe):
            mm, tr = nc.tensor.matmul, nc.tensor.transpose

            pe.sem_inc(S["ada_feat"], 1)
            pe.wait_ge(set_pool, 6)
            pe.wait_ge(set_load[0], 16 * N_ROWS)
            for j in range(NL):
                tr(AUX[0][:, j * 76:(j + 1) * 76], rows[0:76, j, :], ident[0:76, 0:76])
            for j in range(NL):
                last = tr(AUX[1][:, j * 72:(j + 1) * 72], rows[0:72, 2 + j, :], ident[0:72, 0:72])
            last.then_inc(set_pe, 1)
            pe.wait_ge(set_load[1], 32)
            for t in range(2):
                for k in range(KT):
                    last = tr(BK[2 * t + k // 4][:, (k % 4) * P:(k % 4 + 1) * P],
                              stage[:, t, k * P:(k + 1) * P], ident[:, :])
            last.then_inc(set_pe, 1)
            pe.wait_ge(set_load[2], 48)
            pe.wait_ge(set_dve, 2)
            for k in range(KT):
                tr(BK[0][:, k * 8:k * 8 + 8], xc[0:8, 0, k * P:(k + 1) * P], ident[0:8, 0:8])
            for k in range(KT):
                last = tr(BK[1][:, k * 9:k * 9 + 9], xc[0:9, 1, k * P:(k + 1) * P], ident[0:9, 0:9])
            last.then_inc(set_pe, 1)
            pe.wait_ge(set_dve, 4)
            pe.sem_inc(unit_done, SLOTS)

            def ada(L, sub):
                q0 = BASE[f"ada{sub}"] // SLOTS

                def chunk(c, par_):
                    ps = AUX[par_]
                    for s in range(SLOTS):
                        unit_ready(pe, L, q0 + c, s)
                        if s == 0 and not (isinstance(c, int) and c < 2):
                            wait(pe, "ada_row", L, c + (sub * NADA - 2))
                        for k in range(2):
                            kt = s * 2 + k
                            for w in (whi, wlo):
                                last = mm(ps[:, :], cst[:, kt], w[:, s, k * 512:(k + 1) * 512],
                                          start=(kt == 0 and w is whi), stop=(kt == KT - 1 and w is wlo))
                        last.then_inc(unit_done, 1)

                def to_features(c, par_):
                    wait(pe, "ada_row", L, c + sub * NADA)
                    if not (isinstance(c, int) and c == 0):
                        wait(pe, "mod_ready", L, c + (sub * NADA - 1))
                    for j in range(4):
                        last = mm(AUX[2][:, j * 9:j * 9 + 9], ada_row[:, par_, j * P:(j + 1) * P], sel[:, :],
                                  start=True, stop=True)
                    last.then_inc(S["ada_feat"], 1)

                chunk(0, 0)
                wait(pe, "sq_ready", L, sub)
                for k in range(KT):
                    last = mm(AUX[3][:, 0:NT], ones[:, 0:P], tmp[:, k], start=(k == 0), stop=(k == KT - 1))
                last.then_inc(S["ms_done"], 1)
                settle(pe)
                with pe.Fori(0, (NADA - 2) // 2) as i:
                    chunk(i * 2 + 1, 1)
                    to_features(i * 2, 0)
                    chunk(i * 2 + 2, 0)
                    to_features(i * 2 + 1, 1)
                chunk(NADA - 1, 1)
                to_features(NADA - 2, 0)
                to_features(NADA - 1, 1)

            def ffn(L, f):
                sub = 2 * f
                wait(pe, "h_lo", L, sub)
                settle(pe)
                with pe.Fori(0, FT // 2) as i:
                    for s in range(SLOTS):
                        q = BASE[f"in{f}"] // SLOTS + i
                        unit_ready(pe, L, q, s)
                        b = G_BASE[f"in{f}"]
                        e = "AV"[s % 2]
                        n = ev_count(e, b)
                        pe.wait_ge(evac[e], L * EV_TOT[e] + (i * 2 + (n + s // 2 if n or s >= 2 else 1)))
                        for k in range(KT):
                            last = mm3(BK[s][:, 0:NT], s, k * P, hH[:, k], hL[:, k], k == 0, k == KT - 1)
                        last.then_inc(unit_done, 1)
                with pe.Fori(0, 2) as i:
                    for u in range(12):
                        t, part, s = u // 3, u % 3, u % SLOTS
                        unit_ready(pe, L, BASE[f"out{f}"] // SLOTS + i * 3 + u // SLOTS, s)
                        if u == 0:
                            wait(pe, "hid_lo", L, f * FT + 15)
                        if u == 2:
                            wait(pe, "hid_lo", L, f * FT + FT - 1)
                        if part == 0:
                            for e in "AV":
                                n = ev_count(e, G_BASE[f"out{f}"]) + 1
                                pe.wait_ge(evac[e], L * EV_TOT[e] + (n if e == "A" else
                                           (n if t == 0 else n + t - 1) + i * 3))
                        for k in range(OUT_K[part]):
                            kt = part * 8 + k
                            last = mm3(BK[t][:, 0:NT], s, k * P, hidH[:, kt], hidL[:, kt],
                                       kt == 0, kt == FT - 1)
                        last.then_inc(unit_done, 1)

            def level(L, br, li):
                m = LEVELS[li]
                base = 0 if br == "A" else 2
                if m:
                    wait(pe, br + "_mul", L, li - 1)
                if li:
                    wait(pe, br + "_sc", L, li - 1)
                for tile in range(2):
                    if m == 128 and tile == 1:
                        continue
                    for h in range(H):
                        if br == "A":
                            sel_ = lambda t_, h=h: t_[:, h]
                        else:
                            sel_ = lambda t_, h=h: t_[64 * (h % 2):64 * (h % 2) + 64, h // 2]
                        if m == 0:
                            k_, q_ = sel_(K[br]), sel_(Q[br])
                        else:
                            k_ = q_ = sel_(X[br][:, li % 2])
                        s0 = tile * P
                        t0 = P if m == 128 else tile * P
                        bank, col = (tile, h * P) if br == "A" else (h % 2, (h // 2 * 2 + tile) * P)
                        last = mm(AUX[base + bank][:, col:col + P], k_[:, s0:s0 + P], q_[:, t0:t0 + P],
                                  start=True, stop=True)
                last.then_inc(S[br + "_mm"], 1)

            def values_T(L, br):
                base = 0 if br == "A" else 2
                for t in range(2):
                    for h in range(H):
                        last = tr(AUX[base + t][:, h * P:(h + 1) * P], V[br][:, h, t * P:(t + 1) * P], ident[:, :])
                last.then_inc(S[br + "_vT"], 1)

            def sample_T(L, n):
                src = (K["A"], V["A"], K["C"], V["C"])[n]
                if n >= 1:
                    wait(pe, "sTe", L, n - 1)
                for h in range(2 if n == 2 else 4):
                    last = tr(AUX[3][0:NB, h * P:(h + 1) * P], src[:, h, T:NT], ident[:, :])
                last.then_inc(S["sT"], 1)

            def outputs(L, br):
                wait(pe, br + "_sc", L, 8)
                wait(pe, br + "_vTe", L)
                for h in range(H):
                    o = AUX[h // 2][:, (h % 2) * T:(h % 2 + 1) * T]
                    v0, v1 = (VT[br][:, t, h * P:(h + 1) * P] for t in range(2))
                    mm(o, v0, sc[br][:, h, 0:T], start=True, stop=False)
                    last = mm(o[:, P:T], v1, sc[br][:, h, T:T + P], start=False, stop=True)
                last.then_inc(S[br + "_o"], 1)

            def kend_T(L, br):
                wait(pe, br + "_kend", L)
                for t in range(2):
                    for h in range(4 if br == "A" else 2):
                        last = tr(AUX[2 + t][:, h * P:(h + 1) * P], X[br][:, 1, h, t * P:(t + 1) * P], ident[:, :])
                last.then_inc(S[br + "_kT"], 1)

            def final_state(L, br):
                wait(pe, br + "_kTe", L)
                dk = P if br == "A" else 64
                for h in range(H):
                    for t in range(2):
                        last = mm(AUX[2][0:dk, h * P:(h + 1) * P], KTT[:, t, h * dk:(h + 1) * dk],
                                  VT[br][:, t, h * P:(h + 1) * P], start=(t == 0), stop=(t == 1))
                last.then_inc(S[br + "_S"], 1)

            def sample_kv(L, i):
                br, j = BATCHES[i]
                wait(pe, "sTe", L, 3)
                if i == 0:
                    wait(pe, "A_oe", L)
                if i == 4:
                    wait(pe, "C_oe", L)
                if i not in (0, 4):
                    wait(pe, "st_new", L, i - 1)
                for e in range(1 if br == "A" else 2):
                    n = j if br == "A" else 4 + 2 * (j) + e
                    wait(pe, "vblk", L, n)
                    r0 = 0 if br == "A" else 32
                    vb = vblk[n % 2][r0:r0 + NB]
                    for half in range(2):
                        if br == "A":
                            out, kk = AUX[half][:, :], sTs[0:NB, 0, j * P:(j + 1) * P]
                        else:
                            out = AUX[half][64 * e:64 * e + 64, :]
                            kk = sTs[32:32 + NB, 0, j * P + 64 * e:j * P + 64 * e + 64]
                        last = mm(out, kk, vb[:, half * 512:(half + 1) * 512], start=True, stop=True)
                last.then_inc(S["kv"], 1)

            def sample_o(L, i):
                br, j = BATCHES[i]
                wait(pe, "st_new", L, i)
                if i == 0:
                    wait(pe, "A_kTe", L)
                if i == 4:
                    wait(pe, "C_kTe", L)
                    wait(pe, "C_Se", L)
                for e in range(1 if br == "A" else 2):
                    for b in range(NB):
                        if br == "A":
                            w, q_, h = st[:, i % 2, b], Q["A"][:, j, T + b:T + b + 1], j
                        else:
                            r = slice(64 * e, 64 * e + 64)
                            w, q_, h = st[r, i % 2, b], Q["C"][r, j, T + b:T + b + 1], 2 * j + e
                        bank = 3 if br == "A" or e == 0 else 2
                        last = mm(AUX[bank][:, h * NB + b:h * NB + b + 1], w, q_, start=True, stop=True)
                last.then_inc(S["so"], 1)

            def head_ms(L, br):
                wait(pe, br + "_sq", L)
                wait(pe, br + "_Se", L)
                for h in range(H):
                    last = mm(AUX[h][:, 0:NT], ones[:, 0:P], X["A"][:, 0, h],
                              start=True, stop=True)
                last.then_inc(S[br + "_ms"], 1)

            def mixer(L):
                wait(pe, "h_lo", L, 1)
                g = [0]

                def take_bank():
                    bank_free(pe, L, "mix", g[0])
                    g[0] += 1
                    return BK[(g[0] - 1) % 4][:, 0:NT]

                pe.wait_ge(rows_in, (L + 1) * 32)
                settle(pe)
                for j in range(4):
                    tr(AUX[0][:, j * 32:j * 32 + 24], crow[:, j * P:(j + 1) * P], ident[0:24, 0:24])
                    last = tr(AUX[0][:, j * 32 + 24:j * 32 + 32], hrow[:, j * P:(j + 1) * P], ident[0:8, 0:8])
                last.then_inc(S["rowsT"], 1)
                for u, (kind, what, j) in enumerate(MIX):
                    q, s = mix_qs(u)
                    unit_ready(pe, L, q, s)
                    if kind == "in":
                        ps = take_bank()
                        for k in range(KT):
                            last = mm3(ps, s, k * P, hH[:, k], hL[:, k], k == 0, k == KT - 1)
                    elif kind == "ca":
                        if j == 0:
                            ps = take_bank()
                        for k in range(4):
                            last = mm3(ps, s, k * P, hH[:, 4 * j + k], hL[:, 4 * j + k],
                                       k + j == 0, (k, j) == (3, 1))
                    elif kind == "rg":
                        wait(pe, "conv_lo", L)
                        for n in range(4):
                            last = mm3(take_bank(), s, n * P, yH[:, 8 + n], yL[:, 8 + n], True, True)
                    elif kind == "br":
                        y0 = {"a": 0, "b": 4, "c": 8}[what]
                        wait(pe, {"a": "A_lo", "b": "yb_lo", "c": "C_lo"}[what], L)
                        for n in range(2):
                            ps = take_bank()
                            for k in range(4):
                                last = mm3(ps, s, k * 256 + n * P, yH[:, y0 + k], yL[:, y0 + k], k == 0, k == 3)
                    else:
                        ps = take_bank()
                        if j == 0:
                            wait(pe, "m_lo", L, 7)
                        for k in range(KT):
                            last = mm3(ps, s, k * P, yH[:, k], yL[:, k], k == 0, k == KT - 1)
                    last.then_inc(unit_done, 1)
                    if u == 12:
                        wait(pe, "rows_evac", L)
                        evacuated(pe, L, "i", 3)
                        values_T(L, "A")
                    if u == 14:
                        evacuated(pe, L, "ca", 0)
                        pe.wait_ge(wal_in, (L + 1) * 16)
                        for jj in range(2):
                            last = mm(AUX[2][:, jj * 256:jj * 256 + 256], wal[:, jj * P:(jj + 1) * P],
                                      ca[:, 0:256], start=True, stop=True)
                        for jj in range(2):
                            last = mm(AUX[3][:, jj * 8:jj * 8 + 8], wal[:, jj * P:(jj + 1) * P],
                                      ca[:, 256:264], start=True, stop=True)
                        last.then_inc(S["C_alpha"], 1)
                    if u == 15:
                        wait(pe, "A_kk", L)
                        wait(pe, "C_z", L)
                        sample_T(L, 0)
                    if u == 16:
                        wait(pe, "A_vTe", L)
                        sample_T(L, 1)
                    if u == 18:
                        evacuated(pe, L, "ck", 1)
                        sample_T(L, 2)
                    if u == 22:
                        evacuated(pe, L, "cv", 3)
                        sample_T(L, 3)
                    if u == 23:
                        wait(pe, "sTe", L, 3)
                        values_T(L, "C")
                    for li in range(9):
                        if u == PE_LV["A"][li]:
                            level(L, "A", li)
                        if u == PE_LV["C"][li]:
                            if li == 0:
                                wait(pe, "C_vTe", L)
                                wait(pe, "C_cum", L)
                            level(L, "C", li)
                    if u == 53:
                        wait(pe, "C_sc", L, 8)
                        outputs(L, "A")
                        kend_T(L, "A")
                    if u == 54:
                        final_state(L, "A")
                    if 55 <= u < 59:
                        sample_o(L, u - 55)
                    if 54 <= u < 58:
                        sample_kv(L, u - 54)
                    if u == 59:
                        head_ms(L, "A")
                    if u == 61:
                        wait(pe, "A_root", L)
                        outputs(L, "C")
                        kend_T(L, "C")
                    if u == 62:
                        final_state(L, "C")
                    if 63 <= u < 65:
                        sample_o(L, u - 59)
                    if 62 <= u < 64:
                        sample_kv(L, u - 58)
                    if u == 65:
                        head_ms(L, "C")
                    if u == 68:
                        wait(pe, "C_root", L)
                        for jj in range(4):
                            last = tr(AUX[0][0:20, jj * P:(jj + 1) * P], tail[:, jj], ident[:, :])
                        last.then_inc(S["tailT"], 1)

            with pe.Fori(0, NL) as L:
                ada(L, 0)
                ffn(L, 0)
                ada(L, 1)
                mixer(L)
                ada(L, 2)
                ffn(L, 1)

            pe.wait_ge(fin_act, 1)
            for k in range(KT):
                last = mm(AUX[3][:, 0:NT], ones[:, 0:P], tmp[:, k], start=(k == 0), stop=(k == KT - 1))
            last.then_inc(fin_pe, 1)
            pe.wait_ge(fin_dve, 1)
            for t in range(2):
                for k in range(KT):
                    last = tr(BK[2 * t + k // 4][:, (k % 4) * P:(k % 4 + 1) * P], tmp[:, k, t * P:(t + 1) * P],
                              ident[:, :])
            last.then_inc(fin_pe, 1)
            for k in range(KT):
                last = tr(BK[4 + k // 4][0:NB, (k % 4) * P:(k % 4 + 1) * P], tmp[:, k, T:NT], ident[:, :])
            last.then_inc(fin_pe, 1)

        def level_views(br, li):
            m = LEVELS[li]
            r = lambda t_: t_.rearrange("p h (n two m) -> p h n two m", two=2, m=m)
            b = r(B[br][:, :, 0:T])
            e = r(X[br][:, li % 2, :, 0:T])
            shape = [P, 4 if br == "A" else 2, T // (2 * m), m]
            ref = bc(b[:, :, :, 0, m - 1:m], shape)
            return m, r, b, e, ref

        @block.gpsimd
        def _(pool):
            g = nc.gpsimd
            g.memset(ident[:, :], 0.0).then_inc(set_pool, 1)
            pool.wait_ge(set_pool, 1)
            g.affine_select(out=ident[:, :], in_=ident[:, :], compare_op=ALU.not_equal, fill=1.0, base=0,
                            pattern=[[-1, P]], channel_multiplier=1).then_inc(set_pool, 1)
            g.memset(sel[:, :], 0.0).then_inc(set_pool, 1)
            pool.wait_ge(set_pool, 3)
            for n, base in enumerate((0, -32)):
                g.affine_select(out=sel[:, :], in_=sel[:, :], compare_op=ALU.not_equal, fill=1.0, base=base,
                                pattern=[[-1, 9]], channel_multiplier=1).then_inc(set_pool, 1)
                pool.wait_ge(set_pool, 4 + n)
            g.memset(ones[:, :], 1.0)
            g.memset(epst[:, :], EPS)
            g.memset(cst[:, :, :].bitcast(F), 0.0)
            for br in "AC":
                g.memset(sc[br][:, :, :], 0.0)
            g.iota(mask[:, 0, :].bitcast(I32), pattern=[[1, P]], base=0, channel_multiplier=0)
            g.iota(mask[:, 1, :].bitcast(I32), pattern=[[0, P]], base=0, channel_multiplier=1)\
             .then_inc(set_pool, 1)

            def args(L, br, li):
                m, r, b, e, ref = level_views(br, li)
                if li >= 3:
                    wait(pool, br + "_mm", L, li - 2)
                g.tensor_tensor(e[:, :, :, 1], b[:, :, :, 1], ref, ALU.subtract)
                g.tensor_tensor(e[:, :, :, 0], ref, b[:, :, :, 0], ALU.subtract).then_inc(S[br + "_arg"], 1)

            def kend_args(L, br):
                wait(pool, br + "_mm", L, 7)
                n = 4 if br == "A" else 2
                g.tensor_tensor(X[br][:, 1, :, 0:T], bc(B[br][:, :, T - 1:T], [P, n, T]), B[br][:, :, 0:T],
                                ALU.subtract).then_inc(S[br + "_kearg"], 1)

            def st_load(L, i):
                br, j = BATCHES[i]
                if i >= 2:
                    wait(pool, "so", L, i - 2)
                    pool.wait_ge(st_out[i % 2], L * 48 + (i // 2) * 16)
                if br == "A":
                    src = state_hgrn[bass.ds(L, 1), :, j].rearrange("o b d v -> d (o b) v")
                    settle(pool)
                    g.dma_start(st[:, i % 2], src).then_inc(st_in[i % 2], 16)
                else:
                    src = state_gla[bass.ds(L, 1), :, 2 * j:2 * j + 2].rearrange("o b e d v -> e d (o b) v")
                    for e in range(2):
                        settle(pool)
                        g.dma_start(st[64 * e:64 * e + 64, i % 2], src[e]).then_inc(st_in[i % 2], 16)

            def st_in_count(i):
                return 16 * (i // 2 + 1 + (1 if i >= 4 else 0))

            def st_store(L, i):
                br, j = BATCHES[i]
                wait(pool, "st_new", L, i)
                if br == "A":
                    dst = hg_s[bass.ds(L, 1), :, j].rearrange("o b d v -> d (o b) v")
                else:
                    dst = gl_s[bass.ds(L, 1), :, 2 * j:2 * j + 2].rearrange("o b e d v -> (e d) (o b) v")
                settle(pool)
                g.dma_start(dst, st[:, i % 2]).then_inc(st_out[i % 2], 16)

            def v_blocks(L, n):
                r0, h = (0, n) if n < 4 else (32, n - 4)
                if n == 0:
                    wait(pool, "sTe", L, 3)
                    wait(pool, "A_kearg", L)
                if n >= 4:
                    wait(pool, "st_scaled", L, 3 if n < 6 else 4)
                if n >= 2:
                    wait(pool, "kv", L, {2: 0, 3: 1, 4: 2, 5: 3, 6: 4, 7: 4}[n])
                g.tensor_tensor(vblk[n % 2][r0:r0 + NB].rearrange("p (b v) -> p b v", b=NB),
                                bc(sTs[r0:r0 + NB, 1:2, h * P:(h + 1) * P], [NB, NB, P]),
                                bc(ident[r0:r0 + NB, r0:r0 + NB].rearrange("p (b o) -> p b o", o=1), [NB, NB, P]),
                                ALU.mult).then_inc(S["vblk"], 1)

            def scale_state(L, i):
                br, j = BATCHES[i]
                if i == 0:
                    wait(pool, "A_fS", L)
                if i == 4:
                    wait(pool, "C_fS", L)
                if i >= 4:
                    wait(pool, "vblk", L, 2 * i - 3)
                pool.wait_ge(st_in[i % 2], L * 64 + st_in_count(i))
                f = fS[:, i:i + 1, :].rearrange("p o b -> p b o")
                g.tensor_tensor(st[:, i % 2], st[:, i % 2], bc(f, [P, NB, P]), ALU.mult)\
                 .then_inc(S["st_scaled"], 1)

            def mixer(L):
                lx = bass.ds(L, 1)
                wait(pool, "x_ready", L, 0)
                settle(pool)
                g.dma_start(crow[:, 0:512], state_conv[lx].rearrange("o b j d -> (o b j) d")).then_inc(rows_in, 16)
                settle(pool)
                g.dma_start(hrow[:, 0:512], state_rglru[lx].rearrange("o b d -> (o b) d")).then_inc(rows_in, 16)
                settle(pool)
                g.dma_start(wal[:, :], gla_w_alpha[lx].rearrange("o r n -> (o r) n")).then_inc(wal_in, 16)
                settle(pool)
                g.dma_start(cv_s[lx, :, 0:2].rearrange("o b j d -> (o b) (j d)"),
                            state_conv[lx, :, 1:3].rearrange("o b j d -> (o b) (j d)")).then_inc(direct, 16)
                st_load(L, 0)
                st_load(L, 1)
                wait(pool, "A_cum", L)
                order = sorted([(p, br, li) for br in "AC" for li, p in enumerate(PE_LV[br]) if li])
                for n, (p, br, li) in enumerate(order):
                    if br == "C" and li == 1:
                        wait(pool, "C_cum", L)
                    args(L, br, li)
                kend_args(L, "A")
                kend_args(L, "C")
                for i in range(6):
                    if i < 4:
                        v_blocks(L, i)
                    else:
                        v_blocks(L, 2 * i - 4)
                        v_blocks(L, 2 * i - 3)
                    scale_state(L, i)
                    if i >= 1:
                        st_store(L, i - 1)
                    if 1 <= i < 5:
                        st_load(L, i + 1)
                    if i == 2:
                        wait(pool, "A_Se", L)
                        settle(pool)
                        g.dma_start(hg_p[lx, 0].rearrange("o h d v -> d (o h) v"), stF[:, :, :])\
                         .then_inc(fin_out, 16)
                st_store(L, 5)
                wait(pool, "C_Se", L)
                settle(pool)
                g.dma_start(gl_p[lx, 0].rearrange("o h d v -> d (o h) v"), stF[0:64, :, :]).then_inc(fin_out, 16)
                wait(pool, "tail_evac", L)
                settle(pool)
                g.dma_start(cv_p[lx, 0].rearrange("o j d -> (o j) d"), crow[0:3, 0:512]).then_inc(stored, 16)
                settle(pool)
                g.dma_start(cv_s[lx, :, 2].rearrange("o b d -> (o b) d"), crow[3:11, 0:512]).then_inc(stored, 16)
                settle(pool)
                g.dma_start(rl_p[lx, 0], crow[11:12, 0:512]).then_inc(stored, 16)
                settle(pool)
                g.dma_start(rl_s[lx].rearrange("o b d -> (o b) d"), crow[12:20, 0:512]).then_inc(stored, 16)

            with pool.Fori(0, NL) as L:
                mixer(L)
            for i in range(2):
                pool.wait_ge(st_out[i], NL * 48)
            pool.wait_ge(fin_out, NL * 32)
            pool.wait_ge(stored, NL * 64)
            pool.wait_ge(direct, NL * 16)

        @block.scalar
        def _(act):
            def a(out, in_, func, **k):
                return nc.scalar.activation(out, in_, func, **k)

            act.sem_inc(evac["A"], 1)
            act.sem_inc(act_seq, 1)
            for l in range(NL):
                for row, src in row_src[l]:
                    act.dma_start(rows[row:row + src.shape[0], l, :], src).then_inc(set_load[0], 16)
                act.dma_start(rows[0:72, 2 + l, :], b_ada[l].rearrange("(t p) -> t p", p=P)).then_inc(set_load[0], 16)
            for t in range(2):
                act.dma_start(stage[:, t, :], x_prompt[0, t * P:(t + 1) * P, :]).then_inc(set_load[1], 16)
            act.dma_start(xc[0:8, 0, :], x_sample[:, 0, :]).then_inc(set_load[2], 16)
            act.dma_start(xc[0:1, 1, :], c_prompt).then_inc(set_load[2], 16)
            act.dma_start(xc[1:9, 1, :], c_sample).then_inc(set_load[2], 16)
            act.wait_ge(set_dve, 5)
            a(setup_t[:, 0:2, 0:4], setup_t[:, 0:2, 0:4], ACT.Exp).then_inc(set_act, 1)
            a(setup_t[:, 4:6, 0:4], setup_t[:, 4:6, 0:4], ACT.Exp).then_inc(set_act, 1)
            act.wait_ge(set_act, 2)
            a(setup_t[:, 4:6, 0:4], setup_t[:, 4:6, 0:4], ACT.Ln, bias=1.0).then_inc(set_act, 1)
            act.wait_ge(set_dve, 6)
            a(par_all[:, :, PC["L1"]:PC["L1"] + 4], par_all[:, :, PC["L1"]:PC["L1"] + 4], ACT.Ln)
            a(par_all[:, :, PC["l1m"]:PC["l1m"] + 4], par_all[:, :, PC["l1m"]:PC["l1m"] + 4], ACT.Ln)\
                .then_inc(set_act, 1)

            seq = [0]

            def A_(ins):
                ins.then_inc(act_seq, 1)
                seq[0] += 1

            def own(L):
                act.wait_ge(act_seq, L * SEQ + (seq[0] + 1))

            def ada(L, sub, prologue):
                q0 = BASE[f"ada{sub}"] // SLOTS

                def to_row(c, par_, first=False):
                    unit_used(act, L, q0 + c, SLOTS - 1)
                    wait(act, "ada_feat", L, sub * NADA - 1 if first else c + (sub * NADA - 2))
                    a(ada_row[:, par_], AUX[par_][0:64, :], ACT.Copy).then_inc(S["ada_row"], 1)

                for s in range(SLOTS):
                    split_hi(act, L, q0, s)
                wait(act, "x_ready", L, sub - 1)
                a(tmp[:, :, :], x[:, :, :], ACT.Square).then_inc(S["sq_ready"], 1)
                for s in range(SLOTS):
                    split_hi(act, L, q0 + 1, s)
                wait(act, "ms_done", L, sub)
                a(rstd[:, 0], AUX[3][:, 0:NT], ACT.Sqrt, bias=epst[:, 0:1], scale=1.0 / D)\
                    .then_inc(S["root_done"], 1)
                to_row(0, 0, True)
                for s in range(SLOTS):
                    split_hi(act, L, q0 + 2, s)
                to_row(1, 1, True)
                with act.Fori(0, (NADA - 4) // 2) as i:
                    for s in range(SLOTS):
                        split_hi(act, L, i * 2 + (q0 + 3), s)
                    to_row(i * 2 + 2, 0)
                    for s in range(SLOTS):
                        split_hi(act, L, i * 2 + (q0 + 4), s)
                    to_row(i * 2 + 3, 1)
                for s in range(SLOTS):
                    split_hi(act, L, q0 + NADA - 1, s)
                to_row(NADA - 2, 0)
                prologue()
                wait(act, "G_ready", L, sub)
                for k in range(KT):
                    last = a(tmp[:, k, 0:T], tmp[:, k, 0:T], ACT.Identity, scale=Gs[:, k, 0:1],
                             bias=mod[:, sub * 24 + k, 0:1])
                last.then_inc(S["h_p"], 1)
                wait(act, "h_p", L, sub)
                wait(act, "h_s", L, sub)
                a(hH[:, :, :], tmp[:, :, :], ACT.Copy).then_inc(S["h_hi"], 1)
                to_row(NADA - 1, 1)

            def ffn(L, f):
                qi, qo = BASE[f"in{f}"] // SLOTS, BASE[f"out{f}"] // SLOTS
                b = G_BASE[f"in{f}"]

                def step(i, s, ahead):
                    ahead()
                    pair = i * 2 + s // 2
                    if s % 2 == 0:
                        unit_used(act, L, i + qi, s)
                        a(sil[:, s // 2], BK[s][:, 0:NT], ACT.Silu).then_inc(evac["A"], 1)
                    else:
                        act.wait_ge(evac["V"], L * EV_TOT["V"] + (pair + (ev_count("V", b) + 2)))
                        a(hidH[:, bass.ds(pair, 1)].rearrange("p o t -> p (o t)")
                          if not isinstance(pair, int) else hidH[:, pair],
                          hid[:, s // 2], ACT.Copy).then_inc(S["hid_hi"], 1)

                if f == 1:
                    act.wait_ge(stored, (L + 1) * 64)
                    act.wait_ge(fin_out, (L + 1) * 32)
                with act.Fori(0, FT // 2 - 1) as i:
                    for s in range(SLOTS):
                        step(i, s, lambda: split_hi(act, L, i + (qi + (s + 3) // 4), (s + 3) % 4))
                step(FT // 2 - 1, 0, lambda: split_hi(act, L, qi + FT // 2 - 1, 3))
                for s in range(1, SLOTS):
                    step(FT // 2 - 1, s, lambda: split_hi(act, L, qo, s - 1, OUT_K[(s - 1) % 3] * P))
                for u in range(LOOK, U_OUT):
                    split_hi(act, L, qo + u // SLOTS, u % SLOTS, OUT_K[u % 3] * P)

            def mixer(L):
                z, x0, x1, kk = B["A"], X["A"][:, 0], X["A"][:, 1], K["A"]
                EVAC = {
                    "f": (ACT.Copy, lambda j: B["A"][:, j]), "q": (ACT.Silu, lambda j: Q["A"][:, j]),
                    "bx": (ACT.Copy, lambda j: XB[:, j]), "bg": (ACT.Gelu_apprx_tanh, lambda j: XB[:, 4 + j]),
                    "wa": (ACT.Sigmoid, lambda j: tmp[:, 4 + j]), "wx": (ACT.Sigmoid, lambda j: XB[:, j]),
                    "cg": (ACT.Silu, lambda j: GT["C"][:, j]), "ag": (ACT.Silu, lambda j: GT["A"][:, j]),
                    "ma": (ACT.Sigmoid, lambda j: XB[:, j]), "mb": (ACT.Sigmoid, lambda j: sg[:, j % 2]),
                    "mc": (ACT.Sigmoid, lambda j: sg[:, j % 2]),
                }
                for u, (kind, what, j) in enumerate(MIX):
                    if u + LOOK < U_MIX:
                        mix_hi(act, L, u + LOOK)
                    for n, (e, w, t, ug) in enumerate(MG):
                        if ug != u or e != "A":
                            continue
                        unit_used(act, L, *mix_qs(u))
                        if w == "ag":
                            wait(act, "rg_u", L)
                        if w == "wx" or w == "wa":
                            wait(act, "conv_lo", L)
                        if w == "ma":
                            wait(act, "yb_lo", L)
                        if w == "mb" and t >= 2:
                            evacuated(act, L, "brb", t - 2)
                        if w == "mc" and t < 2:
                            evacuated(act, L, "brb", 6 + t)
                        if w == "mc" and t >= 2:
                            evacuated(act, L, "brc", t - 2)
                        fn, dst = EVAC[w]
                        kw = {}
                        if w in ("wa", "wx"):
                            c = PC["rba" if w == "wa" else "rbx"] + t
                            kw = dict(bias=par[:, c:c + 1])
                        a(dst(t), BK[n % 4][:, 0:NT], fn, **kw).then_inc(evac["A"], 1)
                    if u == 5:
                        wait(act, "A_abs", L)
                        A_(a(x1, x1, ACT.Exp))
                        own(L)
                        a(x1, x1, ACT.Ln, bias=1.0).then_inc(S["A_ln"], 1)
                    if u == 7:
                        wait(act, "A_ls", L)
                        a(kk[:, :, :], kk[:, :, :], ACT.Exp).then_inc(S["A_k"], 1)
                    if u == 9:
                        wait(act, "A_diff", L)
                        A_(a(x1, x1, ACT.Exp))
                        own(L)
                        a(x1, x1, ACT.Ln, bias=1.0).then_inc(S["A_ln2"], 1)
                    if u == 11:
                        wait(act, "A_logf", L)
                        a(fS[:, 0:4, :], z[:, :, T:NT], ACT.Exp).then_inc(S["A_fS"], 1)
                    if u == 13:
                        wait(act, "A_vT", L)
                        for t in range(2):
                            last = a(VT["A"][:, t], AUX[t][:, :], ACT.Copy)
                        last.then_inc(S["A_vTe"], 1)
                    if u == 16:
                        c1_ = X["C"][:, 1]
                        wait(act, "C_abs", L)
                        A_(a(c1_, c1_, ACT.Exp))
                        own(L)
                        a(c1_, c1_, ACT.Ln, bias=1.0).then_inc(S["C_ln"], 1)
                    if u == 18:
                        wait(act, "C_logf", L)
                        a(fS[:, 4:6, :], B["C"][:, :, T:NT], ACT.Exp).then_inc(S["C_fS"], 1)
                    if u == 24:
                        wait(act, "C_vT", L)
                        for t in range(2):
                            last = a(VT["C"][:, t], AUX[2 + t][:, :], ACT.Copy)
                        last.then_inc(S["C_vTe"], 1)
                    for br in "AC":
                        for li in range(1, 9):
                            if u == PE_LV[br][li] - 3:
                                wait(act, br + "_arg", L, li - 1)
                                e = X[br][:, li % 2, :, 0:T]
                                a(e, e, ACT.Exp).then_inc(S[br + "_exp"], 1)
                        if u == (50 if br == "A" else 51):
                            wait(act, br + "_kearg", L)
                            e = X[br][:, 1, :, 0:T]
                            a(e, e, ACT.Exp).then_inc(S[br + "_keexp"], 1)
                    if u == 28:
                        wait(act, "conv", L)
                        a(yH[:, 8:12], tmp[:, 0:4], ACT.Copy).then_inc(S["conv_hi"], 1)
                    if u == 32:
                        wait(act, "rg_arg", L)
                        a(tmp[:, 4:8], tmp[:, 4:8], ACT.Tanh).then_inc(S["rg_tanh"], 1)
                    if u == 34:
                        wait(act, "rg_nt", L)
                        a(GT["A"][:, :], GT["A"][:, :], ACT.Sqrt).then_inc(S["rg_sqrt"], 1)
                    if u == 38:
                        wait(act, "yb", L)
                        a(yH[:, 4:8], XB[:, 4:8], ACT.Copy).then_inc(S["yb_hi"], 1)
                    for br, u0 in (("A", 54), ("C", 62)):
                        if u == u0:
                            wait(act, br + "_o", L)
                            for t in range(2):
                                last = a(O[br][:, 2 * t:2 * t + 2, 0:T],
                                         AUX[t][:, :].rearrange("p (h t) -> p h t", h=2), ACT.Copy)
                            last.then_inc(S[br + "_oe"], 1)
                        if u == u0 + 1:
                            wait(act, br + "_S", L)
                            dk = P if br == "A" else 64
                            if br == "C":
                                act.wait_ge(fin_out, L * 32 + 16)
                            a(stF[0:dk], AUX[2][0:dk, :].rearrange("p (h v) -> p h v", h=4), ACT.Copy)\
                                .then_inc(S[br + "_Se"], 1)
                        if u == (59 if br == "A" else 65):
                            wait(act, "so", L, 3 if br == "A" else 5)
                            if br == "A":
                                A_(a(O[br][:, :, T:NT], AUX[3][:, 0:32].rearrange("p (h b) -> p h b", h=4), ACT.Copy))
                            else:
                                for e in range(2):
                                    A_(a(O[br][:, :, T:NT].rearrange("p (j e) b -> p j e b", e=2)[:, :, e],
                                         AUX[3 - e][:, 0:32].rearrange("p (j e b) -> p j e b", j=2, e=2)[:, :, e],
                                         ACT.Copy))
                            own(L)
                            if br == "C":
                                wait(act, "A_lo", L)
                            wait(act, br + "_kTe", L)
                            a(X["A"][:, 0], O[br][:, :, :], ACT.Square).then_inc(S[br + "_sq"], 1)
                            wait(act, br + "_ms", L)
                            for h in range(H):
                                last = a(X["A"][:, 1, h], AUX[h][:, 0:NT], ACT.Sqrt, bias=epst[:, 0:1],
                                         scale=1.0 / P)
                            last.then_inc(S[br + "_root"], 1)
                            wait(act, br + "_y", L)
                            y0 = 0 if br == "A" else 8
                            a(yH[:, y0:y0 + 4], O[br][:, :, :], ACT.Copy).then_inc(S[br + "_hi"], 1)
                    if kind == "br" and what == "c":
                        for n in range(2 * j, 2 * j + 2):
                            wait(act, "mrg", L, n)
                            a(yH[:, n], tmp[:, n], ACT.Copy).then_inc(S["m_hi"], 1)

            with act.Fori(0, NL) as L:
                seq[0] = 0
                wait(act, "layer_par", L)
                for f in range(2):
                    sub = 2 * f
                    ada(L, sub, lambda: [split_hi(act, L, BASE[f"in{f}"] // SLOTS, s) for s in range(LOOK)])
                    ffn(L, f)
                    if f == 0:
                        ada(L, 1, lambda: [mix_hi(act, L, u) for u in range(LOOK)])
                        mixer(L)
                own(L)
                act.sem_inc(act_seq, SEQ - seq[0])

            wait(act, "x_ready", NL, -1)
            a(tmp[:, :, :], x[:, :, :], ACT.Square).then_inc(fin_act, 1)
            act.wait_ge(fin_pe, 1)
            a(rstd[:, 0], AUX[3][:, 0:NT], ACT.Sqrt, bias=epst[:, 0:1], scale=1.0 / D).then_inc(fin_act, 1)
            act.wait_ge(fin_pe, 2)
            for t in range(2):
                for half in range(2):
                    last = a(stage[:, t, half * 512:(half + 1) * 512], BK[2 * t + half][:, :], ACT.Copy)
                last.then_inc(fin_act, 1)
                act.wait_ge(fin_act, 3 + t)
                act.dma_start(y_p[0, t * P:(t + 1) * P, :], stage[:, t, :]).then_inc(y_out, 16)
            act.wait_ge(fin_dve, 2)
            act.dma_start(y_s[:, 0, :], xc[0:NB, 0, :]).then_inc(y_out, 16)
            act.wait_ge(y_out, 48)

        @block.vector
        def _(dve):
            v = nc.vector
            tt = lambda o, i0, i1, op: v.tensor_tensor(o, i0, i1, op)
            ts = lambda o, i, s1, s2, o0, o1: v.tensor_scalar(o, i, s1, s2, o0, o1)

            def neg_abs(out, in_):
                return v.scalar_tensor_tensor(out, in_, -1.0, in_, ALU.mult, ALU.min)

            n0 = [0]

            def st_(ins):
                ins.then_inc(dve_set, 1)
                n0[0] += 1
                dve.wait_ge(dve_set, n0[0])

            dve.wait_ge(set_pool, 6)
            mi = lambda k: mask[:, k, :].bitcast(I32)
            st_(tt(mi(2), mi(0), mi(1), ALU.bitwise_xor))
            st_(tt(mask[:, 3, :], mi(0), mi(1), ALU.is_gt))
            st_(v.tensor_copy(mask[:, 4, :], mi(2)))
            st_(tt(mask[:, 0, :], mask[:, 4, :], mask[:, 3, :], ALU.mult))
            for k in range(7, 0, -1):
                st_(v.tensor_single_scalar(mask[:, k, :], mask[:, 0, :], float(2 ** (k - 1)), ALU.is_ge))
            for k in range(1, 7):
                st_(tt(mask[:, k, :], mask[:, k, :], mask[:, k + 1, :], ALU.subtract))
            st_(v.tensor_copy(mask[:, 0, :], ident[:, :]))
            dve.wait_ge(set_pe, 1)
            st_(v.tensor_copy(par_all[:, :, 0:76], AUX[0][:, 0:152].rearrange("p (l n) -> p l n", l=2)))
            st_(v.tensor_copy(par_all[:, :, 76:148], AUX[1][:, 0:144].rearrange("p (l n) -> p l n", l=2)))
            dve.sem_inc(set_dve, 1)
            dve.wait_ge(set_pe, 2)
            for t in range(2):
                for half in range(2):
                    st_(v.tensor_copy(x[:, half * 4:half * 4 + 4, t * P:(t + 1) * P],
                                      BK[2 * t + half][:, :].rearrange("p (k c) -> p k c", k=4)))
            dve.sem_inc(set_dve, 1)
            dve.wait_ge(set_pe, 3)
            st_(v.tensor_copy(x[:, :, T:NT], BK[0][:, 0:64].rearrange("p (k c) -> p k c", k=KT)))
            c_ps = BK[1][:, 0:72].rearrange("p (k c) -> p k c", k=KT)
            st_(v.tensor_copy(cst[:, :, 0:9], c_ps))
            st_(tt(cst[:, :, 32:41], c_ps, cst[:, :, 0:9].bitcast(F), ALU.subtract))
            dve.sem_inc(lo_done, SLOTS)
            dve.sem_inc(S["x_ready"], 1)
            dve.sem_inc(evac["V"], 1)
            dve.sem_inc(dve_seq, 1)
            dve.sem_inc(set_dve, 2)
            lb = lambda l: par_all[:, 0, PC["lb"] + 4 * l:PC["lb"] + 4 * l + 4]
            s4 = lambda k: setup_t[:, k, 0:4]
            st_(tt(s4(2), lb(0), lb(1), ALU.max))
            for l in range(NL):
                st_(tt(s4(l), lb(l), s4(2), ALU.subtract))
                st_(neg_abs(s4(4 + l), par_all[:, l, PC["lam"]:PC["lam"] + 4]))
            dve.sem_inc(set_dve, 1)
            dve.wait_ge(set_act, 3)
            st_(tt(s4(2), s4(0), s4(1), ALU.add))
            st_(v.reciprocal(s4(2), s4(2)))
            for l in range(NL):
                st_(tt(s4(l), s4(l), s4(2), ALU.mult))
            st_(tt(s4(3), s4(0), s4(1), ALU.add))
            st_(tt(s4(1), s4(3), s4(0), ALU.subtract))
            st_(tt(s4(0), s4(0), s4(0), ALU.subtract))
            for l in range(NL):
                pc = lambda n, l=l: par_all[:, l, PC[n]:PC[n] + 4]
                st_(ts(pc("oml"), s4(l), -1.0, 1.0, ALU.mult, ALU.add))
                st_(v.tensor_single_scalar(pc("L1"), s4(l), 2.0 ** -60, ALU.max))
                st_(v.tensor_single_scalar(pc("l1m"), pc("oml"), 2.0 ** -60, ALU.max))
                st_(ts(s4(6 + l), s4(l), 0.0, -1e30, ALU.is_le, ALU.mult))
                st_(ts(pc("nsp"), par_all[:, l, PC["lam"]:PC["lam"] + 4], -1.0, 0.0, ALU.mult, ALU.max))
                st_(tt(pc("nsp"), pc("nsp"), s4(4 + l), ALU.add))
                st_(v.tensor_single_scalar(pc("nsp"), pc("nsp"), -4.0, ALU.mult))
            dve.sem_inc(set_dve, 1)
            dve.wait_ge(set_act, 4)
            for l in range(NL):
                st_(tt(par_all[:, l, PC["L1"]:PC["L1"] + 4], par_all[:, l, PC["L1"]:PC["L1"] + 4], s4(6 + l),
                       ALU.add))

            seq = [0]

            def V_(ins):
                ins.then_inc(dve_seq, 1)
                seq[0] += 1

            def own(L):
                dve.wait_ge(dve_seq, L * SEQ + (seq[0] + 1))

            def ada(L, sub, prologue):
                q0 = BASE[f"ada{sub}"] // SLOTS

                def to_mod(c):
                    wait(dve, "ada_feat", L, c + sub * NADA)
                    t0 = c * 4 + sub * 24
                    m_ = mod[:, t0:t0 + 4] if isinstance(t0, int) else mod[:, bass.ds(t0, 4)]
                    c0_ = t0 + PC["bada"]
                    b_ = par[:, c0_:c0_ + 4] if isinstance(t0, int) else par[:, bass.ds(c0_, 4)]
                    tt(m_, AUX[2][:, 0:36].rearrange("p (t c) -> p t c", t=4),
                       bc(b_.rearrange("p (t o) -> p t o", o=1), [P, 4, 9]), ALU.add)\
                        .then_inc(S["mod_ready"], 1)

                for c in range(2):
                    for s in range(SLOTS):
                        split_lo(dve, L, q0 + c, s)
                wait(dve, "root_done", L, sub)
                V_(v.reciprocal(rstd[:, 0], rstd[:, 0]))
                own(L)
                V_(tt(tmp[:, :, :], x[:, :, :], bc(rstd[:, :, :], [P, KT, NT]), ALU.mult))
                own(L)
                settle(dve)
                with dve.Fori(0, (NADA - 2) // 2) as i:
                    for par_ in range(2):
                        for s in range(SLOTS):
                            split_lo(dve, L, i * 2 + (q0 + 2 + par_), s)
                        to_mod(i * 2 + par_)
                own(L)
                wait(dve, "mod_ready", L, sub * NADA + 3)
                gain = par[:, PC["gain"] + sub * 8:PC["gain"] + sub * 8 + 8].rearrange("p (k o) -> p k o", o=1)
                v.scalar_tensor_tensor(Gs[:, :, :], mod[:, sub * 24 + 8:sub * 24 + 16, :], 1.0,
                                       bc(gain, [P, KT, 9]), ALU.add, ALU.mult).then_inc(S["G_ready"], 1)
                wait(dve, "G_ready", L, sub)
                V_(tt(tmp[:, :, T:NT], tmp[:, :, T:NT], Gs[:, :, 1:9], ALU.mult))
                own(L)
                tt(tmp[:, :, T:NT], tmp[:, :, T:NT], mod[:, sub * 24:sub * 24 + 8, 1:9], ALU.add)\
                    .then_inc(S["h_s"], 1)
                to_mod(NADA - 2)
                prologue()
                wait(dve, "h_hi", L, sub)
                tt(hL[:, :, :], tmp[:, :, :], hH[:, :, :].bitcast(F), ALU.subtract).then_inc(S["h_lo"], 1)
                to_mod(NADA - 1)
                wait(dve, "mod_ready", L, sub * NADA + 5)
                V_(v.tensor_single_scalar(gate[:, :, :], mod[:, sub * 24 + 16:sub * 24 + 24, :],
                                          1.0 if sub == 1 else 0.5, ALU.mult))

            def add_tile(ps, t):
                v.scalar_tensor_tensor(x[:, t, 0:T], ps[:, 0:T], gate[:, t, 0:1], x[:, t, 0:T], ALU.mult, ALU.add)
                tt(t8[:, t], ps[:, T:NT], gate[:, t, 1:9], ALU.mult).then_inc(evac["V"], 1)

            def add_samples(L, phase, i):
                dve.wait_ge(evac["V"], L * EV_TOT["V"] + (ev_count("V", G_BASE[phase]
                            + (len(MG) if phase == "mix" else KT)) + 1))
                tt(x[:, :, T:NT], x[:, :, T:NT], t8[:, :, :], ALU.add).then_inc(S["x_ready"], 1)

            def ffn(L, f):
                qi, qo = BASE[f"in{f}"] // SLOTS, BASE[f"out{f}"] // SLOTS
                b = G_BASE[f"in{f}"]

                def step(i, s, ahead):
                    ahead()
                    if s % 2 == 0:
                        return
                    pair = i * 2 + s // 2
                    unit_used(dve, L, i + qi, s)
                    dve.wait_ge(evac["A"], L * EV_TOT["A"] + (pair + (ev_count("A", b) + 2)))
                    tt(hid[:, s // 2], sil[:, s // 2], BK[s][:, 0:NT], ALU.mult).then_inc(evac["V"], 1)
                    wait(dve, "hid_hi", L, pair + f * FT)
                    dst, hh = (hidL[:, pair], hidH[:, pair]) if isinstance(pair, int) else (
                        t_[:, bass.ds(pair, 1)].rearrange("p o t -> p (o t)") for t_ in (hidL, hidH))
                    tt(dst, hid[:, s // 2], hh.bitcast(F), ALU.subtract).then_inc(S["hid_lo"], 1)

                if f == 1:
                    dve.wait_ge(stored, (L + 1) * 64)
                    dve.wait_ge(fin_out, (L + 1) * 32)
                    settle(dve)
                with dve.Fori(0, FT // 2 - 1) as i:
                    for s in range(SLOTS):
                        step(i, s, lambda: split_lo(dve, L, i + (qi + (s + 3) // 4), (s + 3) % 4))
                step(FT // 2 - 1, 0, lambda: split_lo(dve, L, qi + FT // 2 - 1, 3))
                for s in range(1, SLOTS):
                    step(FT // 2 - 1, s, lambda: split_lo(dve, L, qo, s - 1, OUT_K[(s - 1) % 3] * P))
                own(L)
                for u in range(U_OUT):
                    w = u + LOOK
                    if w < U_OUT:
                        split_lo(dve, L, qo + w // SLOTS, w % SLOTS, OUT_K[w % 3] * P)
                    if u % 3 == 2:
                        unit_used(dve, L, qo + u // SLOTS, u % SLOTS)
                        add_tile(BK[(u // 3) % 4], u // 3)
                add_samples(L, f"out{f}", 2 * f)

            def mixer(L):
                z, x0, x1, kk = B["A"], X["A"][:, 0], X["A"][:, 1], K["A"]
                zc, c0_, c1_ = B["C"], X["C"][:, 0], X["C"][:, 1]
                cv, r4, bx, bg, t4 = tmp[:, 0:4], tmp[:, 4:8], XB[:, 0:4], XB[:, 4:8], GT["A"]
                pcol = lambda n, j=0: par[:, PC[n] + j:PC[n] + j + 1]

                def conv_tiles(lo_, hi_):
                    for j in range(lo_, hi_):
                        V_(ts(cv[:, j], bx[:, j], pcol("convw", 12 + j), pcol("convb", j), ALU.mult, ALU.add))
                    for d in range(1, 4):
                        own(L)
                        for j in range(lo_, hi_):
                            w = pcol("convw", (3 - d) * 4 + j)
                            V_(v.scalar_tensor_tensor(cv[:, j, d:T], bx[:, j, 0:T - d], w, cv[:, j, d:T],
                                                      ALU.mult, ALU.add))
                            buf = cbuf[:, j, 0:24].rearrange("p (b i) -> p b i", i=3)[:, :, 3 - d]
                            V_(v.scalar_tensor_tensor(cv[:, j, T:NT], buf, w, cv[:, j, T:NT],
                                                      ALU.mult, ALU.add))

                def multiply(br, li):
                    m, r, b, e, ref = level_views(br, li)
                    wait(dve, br + "_exp", L, li - 1)
                    tt(e[:, :, :, 1], e[:, :, :, 1], r(Q[br][:, :, 0:T])[:, :, :, 1], ALU.mult)
                    tt(e[:, :, :, 0], e[:, :, :, 0], r(K[br][:, :, 0:T])[:, :, :, 0], ALU.mult)\
                        .then_inc(S[br + "_mul"], 1)

                def keep(br, li):
                    m = LEVELS[li]
                    wait(dve, br + "_mm", L, li)
                    settle(dve)
                    if br == "C":
                        for e in range(2):
                            ps = AUX[2 + e][:, :].rearrange("p (j t n) -> p j t n", j=2, t=2)
                            dst = sc["C"][:, :, :].rearrange("p (j e) t -> p j e t", e=2)[:, :, e]
                            if m == 128:
                                last = v.tensor_copy(dst[:, :, P:2 * P], ps[:, :, 0])
                                continue
                            for t in range(2):
                                mk = bc(mask[:, li:li + 1, :].bitcast(I32), [P, 2, P])
                                last = v.copy_predicated(dst[:, :, 2 * P * t:2 * P * t + P], mk, ps[:, :, t])
                        last.then_inc(S["C_sc"], 1)
                        return
                    ps = lambda t: AUX[t][:, :].rearrange("p (h t) -> p h t", h=4)
                    if m == 128:
                        last = v.tensor_copy(sc[br][:, :, P:2 * P], ps(0))
                    else:
                        mk = bc(mask[:, li:li + 1, :].bitcast(I32), [P, 4, P])
                        v.copy_predicated(sc[br][:, :, 0:P], mk, ps(0))
                        last = v.copy_predicated(sc[br][:, :, 2 * P:3 * P], mk, ps(1))
                    last.then_inc(S[br + "_sc"], 1)

                for u, (kind, what, j) in enumerate(MIX):
                    if u + LOOK < U_MIX:
                        mix_lo(dve, L, u + LOOK)
                    for n, (e, w, t, ug) in enumerate(MG):
                        if ug != u or e != "V":
                            continue
                        unit_used(dve, L, *mix_qs(u))
                        ps = BK[n % 4][:, 0:NT]
                        if w == "o":
                            own(L)
                            add_tile(ps, t)
                        elif w in ("bra", "brb", "brc"):
                            if w == "brb":
                                evacuated(dve, L, "mb", t)
                                tt(tmp[:, t], sg[:, t % 2], ps, ALU.mult).then_inc(evac["V"], 1)
                            else:
                                s_ = XB[:, t] if w == "bra" else sg[:, t % 2]
                                evacuated(dve, L, "ma" if w == "bra" else "mc", t)
                                own(L)
                                tt(rstd[:, 0], s_, ps, ALU.mult).then_inc(evac["V"], 1)
                                evacuated(dve, L, w, t)
                                last = tt(tmp[:, t], tmp[:, t], rstd[:, 0], ALU.add)
                                if w == "bra":
                                    V_(last)
                                else:
                                    last.then_inc(S["mrg"], 1)
                                    wait(dve, "mrg", L, t)
                        elif w == "ca":
                            v.tensor_copy(ca[:, :], ps[0:16]).then_inc(evac["V"], 1)
                        elif w == "cq":
                            v.tensor_single_scalar(Q["C"][:, t], ps, 64.0 ** -0.5, ALU.mult).then_inc(evac["V"], 1)
                        else:
                            dst = {"i": V["A"], "ck": K["C"], "cv": V["C"]}[w]
                            v.tensor_copy(dst[:, t], ps).then_inc(evac["V"], 1)
                    if u == 0:
                        wait(dve, "rowsT", L)
                        v.tensor_copy(cbuf[:, :, :], AUX[0][:, 0:128].rearrange("p (j c) -> p j c", j=4))\
                            .then_inc(S["rows_evac"], 1)
                    if u == 4:
                        evacuated(dve, L, "f", 3)
                        V_(v.tensor_single_scalar(x0, z[:, :, :], 0.0, ALU.min))
                        neg_abs(x1, z[:, :, :]).then_inc(S["A_abs"], 1)
                    if u == 6:
                        wait(dve, "A_ln", L)
                        V_(tt(x0, x0, x1, ALU.subtract))
                        own(L)
                        tt(kk[:, :, :], x0, z[:, :, :], ALU.subtract).then_inc(S["A_ls"], 1)
                    if u == 8:
                        wait(dve, "A_k", L)
                        for h in range(H):
                            last = v.tensor_scalar(kk[:, h], kk[:, h], pcol("oml", h), None, ALU.mult)
                            V_(ts(x1[:, h], x0[:, h], pcol("l1m", h), pcol("L1", h), ALU.add, ALU.subtract))
                            V_(ts(z[:, h], x0[:, h], pcol("l1m", h), pcol("L1", h), ALU.add, ALU.max))
                            if h == H - 1:
                                last.then_inc(S["A_kk"], 1)
                        own(L)
                        neg_abs(x1, x1).then_inc(S["A_diff"], 1)
                    if u == 10:
                        wait(dve, "A_ln2", L)
                        tt(z[:, :, :], z[:, :, :], x1, ALU.add).then_inc(S["A_logf"], 1)
                    if u == 11:
                        wait(dve, "A_logf", L)
                        wait(dve, "A_fS", L)
                        for h in range(H):
                            last = v.tensor_tensor_scan(z[:, h, 0:T], ones[:, :], z[:, h, 0:T], 0.0,
                                                        ALU.mult, ALU.add)
                        last.then_inc(S["A_cum"], 1)
                    if u == 15:
                        wait(dve, "C_alpha", L)
                        for jj in range(2):
                            V_(v.tensor_scalar(zc[:, jj, 0:T], AUX[2][:, jj * 256:jj * 256 + 256],
                                               pcol("glab", jj), None, ALU.add))
                            last = v.tensor_scalar(zc[:, jj, T:NT], AUX[3][:, jj * 8:jj * 8 + 8],
                                                   pcol("glab", jj), None, ALU.add)
                        last.then_inc(S["C_z"], 1)
                        wait(dve, "C_z", L)
                        own(L)
                        V_(v.tensor_single_scalar(c0_, zc[:, :, :], 0.0, ALU.min))
                        neg_abs(c1_, zc[:, :, :]).then_inc(S["C_abs"], 1)
                    if u == 17:
                        wait(dve, "C_ln", L)
                        V_(tt(c0_, c0_, c1_, ALU.subtract))
                        own(L)
                        v.tensor_single_scalar(zc[:, :, :], c0_, 1.0 / 16.0, ALU.mult).then_inc(S["C_logf"], 1)
                    if u == 18:
                        wait(dve, "C_logf", L)
                        wait(dve, "C_fS", L)
                        for jj in range(2):
                            last = v.tensor_tensor_scan(zc[:, jj, 0:T], ones[:, :], zc[:, jj, 0:T], 0.0,
                                                        ALU.mult, ALU.add)
                        last.then_inc(S["C_cum"], 1)
                    for n, uu in enumerate((16, 17, 19, 23)):
                        if u == uu:
                            wait(dve, "sT", L, n)
                            w_ = 256 if n == 2 else 512
                            r0 = 32 * (n // 2)
                            v.tensor_copy(sTs[r0:r0 + NB, n % 2, 0:w_], AUX[3][0:NB, 0:w_]).then_inc(S["sTe"], 1)
                    for br in "AC":
                        for li in range(9):
                            if li and u == PE_LV[br][li] - 2:
                                multiply(br, li)
                            if u == PE_LV[br][li] + 1:
                                keep(br, li)
                        if u == (51 if br == "A" else 52):
                            wait(dve, br + "_keexp", L)
                            e = X[br][:, 1, :, 0:T]
                            tt(e, e, K[br][:, :, 0:T], ALU.mult).then_inc(S[br + "_kend"], 1)
                    if u == 26:
                        evacuated(dve, L, "bx", 3)
                        conv_tiles(0, 2)
                    if u == 27:
                        conv_tiles(2, 4)
                        own(L)
                        V_(v.tensor_copy(tail[:, :, 0:11], bx[:, :, T - 3:NT]))
                        own(L)
                        dve.sem_inc(S["conv"], 1)
                    if u == 28:
                        wait(dve, "conv_hi", L)
                        tt(yL[:, 8:12], cv, yH[:, 8:12].bitcast(F), ALU.subtract).then_inc(S["conv_lo"], 1)
                    if u == 31:
                        evacuated(dve, L, "wx", 3)
                        V_(tt(bx, bx, cv, ALU.mult))
                        for jj in range(4):
                            last = v.tensor_scalar(r4[:, jj], r4[:, jj], pcol("nsp", jj), None, ALU.mult)
                        last.then_inc(S["rg_arg"], 1)
                    if u == 33:
                        wait(dve, "rg_tanh", L)
                        own(L)
                        ts(t4[:, :, :], r4, -1.0, 1e-34, ALU.mult, ALU.max).then_inc(S["rg_nt"], 1)
                        V_(ts(cv, r4, -1.0, 1.0, ALU.mult, ALU.add))
                        own(L)
                        V_(v.reciprocal(cv, cv))
                    if u == 35:
                        own(L)
                        V_(tt(bx, bx, cv, ALU.mult))
                        V_(v.scalar_tensor_tensor(r4, r4, 1.0, cv, ALU.add, ALU.mult))
                        own(L)
                        wait(dve, "rg_sqrt", L)
                        v.scalar_tensor_tensor(bx, t4[:, :, :], 2.0, bx, ALU.mult, ALU.mult)\
                            .then_inc(S["rg_u"], 1)
                    if u == 36:
                        wait(dve, "rg_u", L)
                        for jj in range(4):
                            V_(v.tensor_tensor_scan(cv[:, jj, 0:T], r4[:, jj, 0:T], bx[:, jj, 0:T], 0.0,
                                                    ALU.mult, ALU.add))
                        V_(tt(cv[:, :, T:NT], r4[:, :, T:NT], cbuf[:, :, 24:32], ALU.mult))
                        own(L)
                        V_(tt(cv[:, :, T:NT], cv[:, :, T:NT], bx[:, :, T:NT], ALU.add))
                    if u == 37:
                        own(L)
                        V_(v.tensor_copy(tail[:, :, 11:20], cv[:, :, T - 1:NT]))
                        evacuated(dve, L, "bg", 3)
                        tt(bg, bg, cv, ALU.mult).then_inc(S["yb"], 1)
                    if u == 38:
                        wait(dve, "yb_hi", L)
                        tt(yL[:, 4:8], bg, yH[:, 4:8].bitcast(F), ALU.subtract).then_inc(S["yb_lo"], 1)
                        own(L)
                    if u == 53:
                        wait(dve, "A_kT", L)
                        for t in range(2):
                            last = v.tensor_copy(KTT[:, t], AUX[2 + t][:, :])
                        last.then_inc(S["A_kTe"], 1)
                    if u == 61:
                        wait(dve, "C_kT", L)
                        for t in range(2):
                            last = v.tensor_copy(KTT[:, t, 0:256], AUX[2 + t][:, 0:256])
                        last.then_inc(S["C_kTe"], 1)
                    for i, uu in enumerate((54, 55, 56, 57, 62, 63)):
                        if u == uu:
                            wait(dve, "kv", L, i)
                            wait(dve, "st_scaled", L, i)
                            for half in range(2):
                                h4 = slice(4 * half, 4 * half + 4)
                                last = tt(st[:, i % 2, h4], st[:, i % 2, h4],
                                          AUX[half][:, :].rearrange("p (b v) -> p b v", b=4), ALU.add)
                            last.then_inc(S["st_new"], 1)
                    for br, uu, y0 in (("A", 59, 0), ("C", 65, 8)):
                        if u == uu:
                            wait(dve, br + "_root", L)
                            r_ = X["A"][:, 1]
                            V_(v.reciprocal(r_, r_))
                            own(L)
                            V_(v.scalar_tensor_tensor(O[br][:, :, :], O[br][:, :, :],
                                                      pcol("hnorm" if br == "A" else "gnorm"), r_,
                                                      ALU.mult, ALU.mult))
                            own(L)
                            evacuated(dve, L, "ag" if br == "A" else "cg", 3)
                            tt(O[br][:, :, :], O[br][:, :, :], GT[br][:, :, :], ALU.mult).then_inc(S[br + "_y"], 1)
                            wait(dve, br + "_hi", L)
                            tt(yL[:, y0:y0 + 4], O[br][:, :, :], yH[:, y0:y0 + 4].bitcast(F), ALU.subtract)\
                                .then_inc(S[br + "_lo"], 1)
                    if kind == "br" and what == "c":
                        for n in range(2 * j, 2 * j + 2):
                            wait(dve, "m_hi", L, n)
                            tt(yL[:, n], tmp[:, n], yH[:, n].bitcast(F), ALU.subtract).then_inc(S["m_lo"], 1)
                    if u == 69:
                        wait(dve, "tailT", L)
                        v.tensor_copy(crow[0:20, 0:512], AUX[0][0:20, :]).then_inc(S["tail_evac"], 1)
                add_samples(L, "mix", 1)

            with dve.Fori(0, NL) as L:
                seq[0] = 0
                src = par_all[:, bass.ds(L, 1), :].rearrange("p o n -> p (o n)")
                v.tensor_copy(par[:, :], src).then_inc(S["layer_par"], 1)
                wait(dve, "layer_par", L)
                for f in range(2):
                    ada(L, 2 * f, lambda: [split_lo(dve, L, BASE[f"in{f}"] // SLOTS, s) for s in range(LOOK)])
                    ffn(L, f)
                    if f == 0:
                        ada(L, 1, lambda: [mix_lo(dve, L, u) for u in range(LOOK)])
                        mixer(L)
                own(L)
                assert seq[0] <= SEQ
                dve.sem_inc(dve_seq, SEQ - seq[0])

            dve.wait_ge(fin_act, 2)
            st_(v.reciprocal(rstd[:, 0], rstd[:, 0]))
            st_(tt(tmp[:, :, :], x[:, :, :], bc(rstd[:, :, :], [P, KT, NT]), ALU.mult))
            fn = par[:, PC["fnorm"]:PC["fnorm"] + 8].rearrange("p (k o) -> p k o", o=1)
            tt(tmp[:, :, :], tmp[:, :, :], bc(fn, [P, KT, NT]), ALU.mult).then_inc(fin_dve, 1)
            dve.wait_ge(fin_pe, 3)
            for half in range(2):
                last = v.tensor_copy(xc[0:NB, 0, half * 512:(half + 1) * 512], BK[4 + half][0:NB, :])
            last.then_inc(fin_dve, 1)


_INS = ['x_prompt', 'x_sample', 'c_prompt', 'c_sample', 'state_hgrn', 'state_conv', 'state_rglru', 'state_gla',
        'w_ada', 'b_ada', 'norm_gain', 'w_ffn_in', 'w_ffn_out', 'w_in', 'hgrn_lb_logits', 'hgrn_norm', 'conv_w',
        'conv_b', 'rg_wa', 'rg_ba', 'rg_wx', 'rg_bx', 'rg_lambda', 'gla_w_alpha', 'gla_b_alpha', 'gla_norm',
        'w_br_a', 'w_br_b', 'w_br_c', 'w_out', 'final_norm']
_OUTS = [(1, T, D), (NB, 1, D), (NL, 1, 4, 128, 128), (NL, NB, 4, 128, 128), (NL, 1, 3, 512), (NL, NB, 3, 512),
         (NL, 1, 512), (NL, NB, 512), (NL, 1, 4, 64, 128), (NL, NB, 4, 64, 128)]


def kernel(**inputs):
    import numpy as _np
    import concourse.bacc as _bacc
    from concourse.bass_utils import run_bass_kernel_spmd as _run

    nc = _bacc.Bacc("TRN2", target_bir_lowering=False, num_devices=1, dynamic_dma_scratch_size=SCRATCH)
    arrays, args = {}, []
    for name in _INS:
        a = _np.ascontiguousarray(inputs[name])
        arrays[f"in_{name}"] = a
        args.append(nc.dram_tensor(f"in_{name}", a.shape, mybir.dt.from_np(a.dtype), kind="ExternalInput").ap())
    for i, shape in enumerate(_OUTS):
        args.append(nc.dram_tensor(f"out_{i}", shape, F, kind="ExternalOutput").ap())
    trunk(nc, *args)
    r = _run(nc, [arrays], core_ids=[0])
    return tuple(r.results[0][f"out_{i}"] for i in range(len(_OUTS)))
```

```python
import concourse.bass as bass
from concourse import mybir
from contextlib import ExitStack

F = mybir.dt.float32
FR = mybir.dt.float32r
I32 = mybir.dt.int32
ACT = mybir.ActivationFunctionType
ALU = mybir.AluOpType

P = 128
D = 1024
KT = D // P
T, NB = 256, 8
NT = T + NB
NL = 2
FFN = 2816
FT = FFN // P
H = 4
EPS = 1e-6
SLOTS, UC = 4, 1024
ADA_C = 512
NADA = 3 * D // ADA_C

U_ADA, U_IN, U_MIX = 4 * NADA, 2 * FT, 84 + 4 * NADA
OUT_K = (8, 8, 6)


def out_units(f):
    out = []
    for n in range(12):
        if f == 0:
            out.append(("a", n // 4, n % 4))
        out.append(("o", n // 3, n % 3))
    return out


OUT_SEQ = [out_units(0), out_units(1)]
U_OUT = [2 * len(q) for q in OUT_SEQ]
BASE = {}
_at = 0
for _name, _n in (("ada0", U_ADA), ("in0", U_IN), ("out0", U_OUT[0]), ("mix", U_MIX), ("in1", U_IN),
                  ("out1", U_OUT[1])):
    BASE[_name] = _at
    _at += _n
UNITS = _at
ADA_PAR = (0, 1, 0)
HEAD = dict(ms=1, root=2, inverse=2, spread=3, scaled=4, high=5, low=5)
WARM = 10
LOOK = 3

C_AQ, C_AF, C_AI, C_AG, C_BX, C_BG = 0, 512, 1024, 1536, 2048, 2560
C_CQ, C_CK, C_CV, C_CG, C_CA, C_MA, C_MB, C_MC = 3072, 3328, 3584, 4096, 4608, 4624, 5648, 6672


def mixer_units():
    out = []
    for kind, n in (("f", 4), ("q", 4), ("i", 4)):
        out += [("in", kind, j) for j in range(n)]
    out += [("ca", "ca", 0), ("ca", "ca", 1)]
    for kind, n in (("cq", 2), ("ck", 2), ("cv", 4), ("bx", 4), ("bg", 4)):
        out += [("in", kind, j) for j in range(n)]
    out += [("rg", "wa", 0), ("rg", "wx", 0)]
    for kind, n in (("cg", 4), ("ag", 4), ("ma", 8)):
        out += [("in", kind, j) for j in range(n)]
    for j in range(4):
        out += [("in", "mb", 2 * j), ("in", "mb", 2 * j + 1), ("br", "b", j)]
    out += [("br", "a", j) for j in range(4)]
    for j in range(4):
        out += [("in", "mc", 2 * j), ("in", "mc", 2 * j + 1), ("br", "c", j)]
    out += [("out", "o", j) for j in range(8)]
    return out


FILL = {30: 1, 31: 1, 59: 2, 65: 2}
MIX, OLD = [], []
for _o, _unit in enumerate(mixer_units()):
    MIX.append(_unit)
    OLD.append(_o)
    for _ in range(FILL.get(_o, 0)):
        _c = OLD.count(-1) // 4
        MIX += [("ada", _c, _s) for _s in range(4)]
        OLD += [-1] * 4
assert len(MIX) == U_MIX


def at(o, k=0):
    return OLD.index(o) + k


COLS = dict(f=C_AF, q=C_AQ, i=C_AI, cq=C_CQ, ck=C_CK, cv=C_CV, bx=C_BX, bg=C_BG, cg=C_CG, ag=C_AG,
            ma=C_MA, mb=C_MB, mc=C_MC)
BY_ACT = {"f", "bx", "bg", "wa", "wx", "ma", "mb", "mc"}


def mixer_groups():
    out = []
    for u, (kind, what, j) in enumerate(MIX):
        e = "A" if what in BY_ACT else "V"
        if kind in ("in", "out"):
            out.append((e, what, j, u))
        elif kind == "ada" and j == 0:
            out.append(("A", "ada", what, u + 3))
        elif kind == "ca" and j == 1:
            out.append((e, what, 0, u))
        elif kind == "rg":
            out += [(e, what, n, u) for n in range(4)]
        elif kind == "br":
            out += [(e, "br" + what, 2 * j + n, u) for n in range(2)]
        if MIX[u - 2][0] == "ada" and MIX[u - 2][2] == 3:
            out.append(("V", "adaf", MIX[u - 2][1], u))
    return out


MG = mixer_groups()
GI = {(what, j): n for n, (_, what, j, _) in enumerate(MG)}
EV_IN, EV_OUT, EV_MIX = "AV" * FT, "V" * KT, "".join(g[0] for g in MG)
EV = EV_IN + EV_OUT + EV_MIX + EV_IN + EV_OUT
G_BASE = {"in0": 0, "out0": 2 * FT, "mix": 2 * FT + KT, "in1": 2 * FT + KT + len(MG),
          "out1": 4 * FT + KT + len(MG)}
EV_TOT = {e: EV.count(e) for e in "AV"}


def ev_count(e, g):
    return EV[:g].count(e)


SCRATCH = 4096
PC = dict(gain=0, convw=24, convb=40, rba=44, rbx=48, lam=52, glab=56, hnorm=58, gnorm=59, lb=60,
          fnorm=68, bada=76, L1=148, l1m=152, oml=156, nsp=160)
NPAR = 164

LEVELS = [0, 1, 2, 4, 8, 16, 32, 64, 128]

PE_LV = {"A": [16 + 4 * i for i in range(9)], "C": [25 + 3 * i for i in range(9)]}
BATCHES = [("A", 0), ("A", 1), ("A", 2), ("A", 3), ("C", 0), ("C", 1)]


def trunk(nc, x_prompt, x_sample, c_prompt, c_sample, state_hgrn, state_conv, state_rglru, state_gla,
          w_ada, b_ada, norm_gain, w_ffn_in, w_ffn_out, w_in, hgrn_lb_logits, hgrn_norm, conv_w,
          conv_b, rg_wa, rg_ba, rg_wx, rg_bx, rg_lambda, gla_w_alpha, gla_b_alpha, gla_norm, w_br_a,
          w_br_b, w_br_c, w_out, final_norm, y_p, y_s, hg_p, hg_s, cv_p, cv_s, rl_p, rl_s, gl_p, gl_s):
    ctx = ExitStack()
    with ctx:
        def sem(name):
            return ctx.enter_context(nc.semaphore(name))

        def sb(name, shape, dt=F, c=ctx):
            return c.enter_context(nc.sbuf_tensor(name, shape, dt))

        raw = sb("raw", [P, SLOTS, UC])
        whi = sb("whi", [P, SLOTS, UC], FR)
        wlo = sb("wlo", [P, SLOTS, UC], FR)
        x = sb("x", [P, KT, NT])
        hH = sb("hH", [P, KT, NT], FR)
        hL = sb("hL", [P, KT, NT], FR)
        tmp = sb("tmp", [P, KT, NT])
        mod = sb("mod", [P, 72, 9])
        Gs = sb("Gs", [P, KT, 9])
        gate = sb("gate", [P, KT, 9])
        par_all = sb("par_all", [P, NL, NPAR])
        par = sb("par", [P, NPAR])
        cst = sb("cst", [P, KT, P], FR)
        ident = sb("ident", [P, P])
        ones = sb("ones", [P, T])
        sel = sb("sel", [64, 9])
        mask = sb("mask", [P, 8, P])
        ada_row = sb("ada_row", [64, 2, ADA_C])
        rstd = sb("rstd", [P, 1, NT])
        t8 = sb("t8", [P, KT, NB])
        epst = sb("epst", [P, 1])
        scrap = sb("scrap", [P, 1])
        onecol = sb("onecol", [P, 2 * H - 1])
        sc = {"A": sb("scA", [P, H, 384]), "C": sb("scC", [P, H, 384])}
        VTA = sb("VTA", [P, 2, 512])
        st = sb("st", [P, 2, NB, P])
        vblk1 = sb("vblk1", [40, NB * P])
        sTs = sb("sTs", [40, 2, 512])
        wal = sb("wal", [16, 256])
        tail = sb("tail", [P, 4, 20])
        cbuf = sb("cbuf", [P, 4, 32])
        fS = sb("fS", [P, 6, NB])
        with ExitStack() as c0:
            stage = sb("stage", [P, 2, D], c=c0)
            xc = sb("xc", [16, 2, D], c=c0)
            rows = sb("rows", [P, 4, P], c=c0)
            setup_t = sb("setup_t", [P, 8, 16], c=c0)
        with ExitStack() as c1:
            hidH = sb("hidH", [P, FT, NT], FR, c=c1)
            hidL = sb("hidL", [P, FT, NT], FR, c=c1)
            sil = sb("sil", [P, 2, NT], c=c1)
            hid = sb("hid", [P, 2, NT], c=c1)
        c2 = ctx.enter_context(ExitStack())
        yH = sb("yH", [P, 12, NT], FR, c=c2)
        yL = sb("yL", [P, 12, NT], FR, c=c2)
        B = {"A": sb("bA", [P, 4, NT], c=c2), "C": sb("bC", [P, 2, NT], c=c2)}
        Q = {"A": sb("qA", [P, 4, NT], c=c2), "C": sb("qC", [P, 2, NT], c=c2)}
        K = {"A": sb("kA", [P, 4, NT], c=c2), "C": sb("kC", [P, 2, NT], c=c2)}
        V = {"A": sb("vA", [P, 4, NT], c=c2), "C": sb("vC", [P, 4, NT], c=c2)}
        GT = {"A": sb("gA", [P, 4, NT], c=c2), "C": sb("gC", [P, 4, NT], c=c2)}
        ca = sb("ca", [16, NT], c=c2)
        XB = sb("XB", [P, 8, NT], c=c2)
        X = {"A": sb("xA", [P, 2, 4, NT], c=c2), "C": sb("xC", [P, 2, 2, NT], c=c2)}
        sg = sb("sg", [P, 2, NT], c=c2)
        flat = lambda t_: t_[:, :, :].rearrange("p k t -> p (k t)")
        O = {"A": Q["A"], "C": V["C"]}
        VT = {"A": VTA, "C": flat(V["A"])[:, 0:D].rearrange("p (t n) -> p t n", t=2)}
        KTT = flat(K["A"])[:, 0:D].rearrange("p (t n) -> p t n", t=2)
        vblk = [flat(B["A"])[:, 0:D], vblk1[:, :]]
        stF = flat(B["C"])[:, 0:H * P].rearrange("p (h v) -> p h v", h=H)
        crow, hrow = X["A"][0:24, 0, 0:2].rearrange("p k t -> p (k t)"), X["A"][0:NB, 1, 0:2].rearrange("p k t -> p (k t)")
        BK = [ctx.enter_context(nc.psum_tensor(f"bank{i}", [P, 512], F)) for i in range(8)]
        AUX = BK[4:]

        landed = [sem(f"landed{i}") for i in range(SLOTS)]
        hi_done = sem("hi_done")
        lo_done = sem("lo_done")
        unit_done = sem("unit_done")
        evac = {"A": sem("evac_act"), "V": sem("evac_dve")}
        PER = {}
        S = {}

        def event(name, per=1):
            S[name], PER[name] = sem(name), per

        for name, per in (
                ("layer_par", 1), ("ada_row", 2 * NADA), ("ada_feat", 3 * NADA),
                ("mod_ready", 2 * NADA), ("sq_ready", 3 * KT), ("ms_done", 3), ("root_done", 3),
                ("xn_ready", 12), ("G_ready", 3), ("h_p", 12), ("h_s", 3), ("h_hi", 12), ("h_lo", 12),
                ("hid_hi", 2 * FT), ("hid_lo", 2 * FT), ("x_ready", 3 * KT),
                ("state_rows", 1), ("rowsT", 1), ("rows_evac", 1),
                ("A_abs", 1), ("C_abs", 1), ("C_logf", 1), ("A_kearg", 1), ("C_kearg", 1), ("A_keexp", 1), ("C_keexp", 1), ("rg_u", 1), ("A_ln", 1), ("A_ls", 1), ("A_k", 1), ("A_diff", 1),
                ("A_ln2", 1), ("A_logf", 1), ("A_cum", 1), ("A_fS", 1), ("C_fS", 1), ("A_kend", 1), ("C_kend", 1),
                ("A_kk", 1), ("C_alpha", 1), ("C_z", 1), ("C_ln", 1), ("C_cum", 1),
                ("A_arg", 8), ("A_exp", 8), ("A_mul", 8), ("A_mm", 9), ("A_sc", 9),
                ("C_arg", 8), ("C_exp", 8), ("C_mul", 8), ("C_mm", 9), ("C_sc", 9),
                ("A_vT", 1), ("A_vTe", 1), ("C_vT", 1), ("C_vTe", 1),
                ("sT", 4), ("sTe", 4),
                ("conv", 1), ("conv_hi", 1), ("conv_lo", 1), ("rg_arg", 1), ("rg_tanh", 1), ("rg_nt", 1),
                ("rg_sqrt", 1), ("yb", 1), ("yb_hi", 1), ("yb_lo", 1), ("tailT", 1), ("tail_evac", 1), ("xb_free", 1),
                ("A_o", 1), ("A_oe", 1), ("C_o", 1), ("C_oe", 1),
                ("A_kT", 1), ("A_kTe", 1), ("C_kT", 1), ("C_kTe", 1),
                ("A_S", 1), ("A_Se", 1), ("C_S", 1), ("C_Se", 1),
                ("vblk", 8), ("kv", 6), ("st_new", 6), ("so", 6), ("A_soe", 1), ("C_soe", 1),
                ("A_sq", 1), ("A_w", 1), ("A_ms", 1), ("A_root", 1), ("A_y", 1), ("A_hi", 1), ("A_lo", 1),
                ("C_sq", 1), ("C_w", 1), ("A_rec", 1), ("C_rec", 1), ("A_spread", 1), ("C_spread", 1), ("C_ms", 1), ("C_root", 1), ("C_y", 1), ("C_hi", 1), ("C_lo", 1),
                ("mrg", 8), ("g_tanh", 12), ("m_hi", 8), ("m_lo", 8)):
            event(name, per)
        st_in = [sem(f"st_in{i}") for i in range(2)]
        st_out = [sem(f"st_out{i}") for i in range(2)]
        fin_out = sem("fin_out")
        stored = sem("stored")
        direct = sem("direct")
        rows_in = sem("rows_in")
        set_onecol = sem("set_onecol")
        set_mask = sem("set_mask")
        wal_in = sem("wal_in")
        dve_set = sem("dve_set")
        dve_seq = sem("dve_seq")
        act_seq = sem("act_seq")
        set_load = [sem(f"set_load{i}") for i in range(3)]
        set_pool, set_pe, set_dve, set_act = (sem(n) for n in ("set_pool", "set_pe", "set_dve", "set_act"))
        fin_dve, fin_act, fin_pe, y_out = (sem(n) for n in ("fin_dve", "fin_act", "fin_pe", "y_out"))
        CREDIT = {"x_ready": KT, "sq_ready": KT, "ada_feat": 2, "mod_ready": 1, "ada_row": 1}
        settled = sem("settled")
        SEQ = 512

        def wait(eng, name, L, i=0):
            eng.wait_ge(S[name], L * PER[name] + (i + (1 + CREDIT.get(name, 0))))

        def settle(eng):
            eng.sem_inc(settled, 1)

        def unit_no(L, q, s):
            return L * UNITS + q * SLOTS + s

        def bc(ap, shape):
            return ap.broadcast_to(shape)

        def load(sp, L, q, s, dst_shape, src):
            sp.wait_ge(lo_done, unit_no(L, q, s) + 1)
            settle(sp)
            sp.dma_start(dst_shape, src).then_inc(landed[s], 16)

        def split_hi(act, L, q, s, n=UC):
            act.wait_ge(landed[s], (L * (UNITS // SLOTS) + q + 1) * 16)
            act.wait_ge(unit_done, unit_no(L, q, s) + 1)
            nc.scalar.activation(whi[:, s, 0:n], raw[:, s, 0:n], ACT.Copy).then_inc(hi_done, 1)

        def split_lo(dve, L, q, s, n=UC):
            dve.wait_ge(hi_done, unit_no(L, q, s) + 1)
            nc.vector.tensor_tensor(wlo[:, s, 0:n], raw[:, s, 0:n], whi[:, s, 0:n].bitcast(F),
                                    ALU.subtract).then_inc(lo_done, 1)

        def unit_ready(pe, L, q, s):
            pe.wait_ge(lo_done, unit_no(L, q, s) + 1 + SLOTS)

        def unit_used(eng, L, q, s):
            eng.wait_ge(unit_done, unit_no(L, q, s) + 1 + SLOTS)

        def mm3(out, s, col, rh, rl, start, stop):
            a, b = whi[:, s, col:col + P], wlo[:, s, col:col + P]
            nc.tensor.matmul(out, a, rh, start=start, stop=False)
            nc.tensor.matmul(out, a, rl, start=False, stop=False)
            return nc.tensor.matmul(out, b, rh, start=False, stop=stop)

        def bank_free(pe, L, phase, g):
            b = G_BASE[phase]
            if g == 0:
                for e in "AV":
                    pe.wait_ge(evac[e], L * EV_TOT[e] + (ev_count(e, b) + 1))
            elif g >= 4:
                e = EV[b + g - 4]
                pe.wait_ge(evac[e], L * EV_TOT[e] + (ev_count(e, b + g - 3) + 1))

        def st_in_count(i):
            return 16 * (i // 2 + 1 + (1 if i >= 4 else 0))

        def mix_qs(u):
            return BASE["mix"] // SLOTS + u // SLOTS, u % SLOTS

        def mix_cols(u):
            return 512 if MIX[u][0] in ("ca", "rg") else UC

        def evacuated(eng, L, what, j):
            g = GI[(what, j)]
            e = MG[g][0]
            eng.wait_ge(evac[e], L * EV_TOT[e] + (ev_count(e, G_BASE["mix"] + g + 1) + 1))

        def mix_hi(act, L, u):
            split_hi(act, L, *mix_qs(u), mix_cols(u))

        def mix_lo(dve, L, u):
            split_lo(dve, L, *mix_qs(u), mix_cols(u))

        def out_qs(f, i, k):
            return BASE[f"out{f}"] // SLOTS + i * (len(OUT_SEQ[f]) // SLOTS) + k // SLOTS, k % SLOTS

        def out_cols(f, k):
            kind, _, part = OUT_SEQ[f][k % len(OUT_SEQ[f])]
            return OUT_K[part] * P if kind == "o" else UC

        row_src = []
        for l in range(NL):
            row_src.append([
                (PC["gain"], norm_gain[l].rearrange("s (k p) -> (s k) p", p=P)),
                (PC["convw"], conv_w[l].rearrange("j (k p) -> (j k) p", p=P)),
                (PC["convb"], conv_b[l].rearrange("(k p) -> k p", p=P)),
                (PC["rba"], rg_ba[l].rearrange("(k p) -> k p", p=P)),
                (PC["rbx"], rg_bx[l].rearrange("(k p) -> k p", p=P)),
                (PC["lam"], rg_lambda[l].rearrange("(k p) -> k p", p=P)),
                (PC["glab"], gla_b_alpha[l].rearrange("(k p) -> k p", p=P)),
                (PC["hnorm"], hgrn_norm[l:l + 1, :]),
                (PC["gnorm"], gla_norm[l:l + 1, :]),
                (PC["lb"], hgrn_lb_logits.rearrange("l (k p) -> (l k) p", p=P)),
                (PC["fnorm"], final_norm.rearrange("(k p) -> k p", p=P)),
            ])
        N_ROWS = sum(len(r) for r in row_src) + NL

        block = ctx.enter_context(nc.Block())

        @block.sync
        def _(sp):
            r3 = lambda ap, k: ap.rearrange("p (k n) -> p k n", k=k)

            def ada_load(L, q, slot, sub, c, s):
                src = w_ada[bass.ds(L, 1), s * 256:(s + 1) * 256, bass.ds(c * ADA_C + sub * 3 * D, ADA_C)]
                load(sp, L, q, slot, r3(raw[:, slot], 2), src.rearrange("o (k p) n -> p (o k) n", p=P))

            def ffn(L, f):
                with sp.Fori(0, FT // 2) as i:
                    for s in range(SLOTS):
                        col = (i * 2 + s // 2) * P + (s % 2) * FFN
                        src = w_ffn_in[bass.ds(L, 1), f, :, bass.ds(col, P)]
                        load(sp, L, BASE[f"in{f}"] // SLOTS + i, s, r3(raw[:, s], KT),
                             src.rearrange("o (k p) n -> p (o k) n", p=P))
                with sp.Fori(0, 2) as i:
                    for k, (kind, t, part) in enumerate(OUT_SEQ[f]):
                        q, s = out_qs(f, i, k)
                        if kind == "a":
                            ada_load(L, q, s, 1, i * 3 + t, part)
                            continue
                        src = w_ffn_out[bass.ds(L, 1), f, part * 8 * P:(part * 8 + OUT_K[part]) * P,
                                        bass.ds((i * 4 + t) * P, P)]
                        load(sp, L, q, s, r3(raw[:, s, 0:OUT_K[part] * P], OUT_K[part]),
                             src.rearrange("o (k p) n -> p (o k) n", p=P))

            def mixer(L):
                for u, (kind, what, j) in enumerate(MIX):
                    q, s = mix_qs(u)
                    lx = bass.ds(L, 1)
                    if kind == "ada":
                        ada_load(L, q, s, 2, what, j)
                        continue
                    if kind == "in":
                        c = COLS[what] + j * P
                        dst, src = r3(raw[:, s], KT), w_in[lx, :, c:c + P]
                    elif kind == "ca":
                        dst, src = r3(raw[:, s, 0:512], 4), w_in[lx, j * 512:(j + 1) * 512, C_CA:C_CA + P]
                    elif kind == "rg":
                        w = rg_wa if what == "wa" else rg_wx
                        load(sp, L, q, s, r3(raw[:, s, 0:512], 4), w[lx].rearrange("o n k j -> k (o n) j"))
                        continue
                    elif kind == "br":
                        w = {"a": w_br_a, "b": w_br_b, "c": w_br_c}[what]
                        dst, src = r3(raw[:, s], 4), w[lx, :, j * 256:(j + 1) * 256]
                    else:
                        dst, src = r3(raw[:, s], KT), w_out[lx, :, j * P:(j + 1) * P]
                    load(sp, L, q, s, dst, src.rearrange("o (k p) n -> p (o k) n", p=P))

            with sp.Fori(0, NL) as L:
                with sp.Fori(0, NADA) as c:
                    for s in range(SLOTS):
                        ada_load(L, BASE["ada0"] // SLOTS + c, s, 0, c, s)
                ffn(L, 0)
                mixer(L)
                ffn(L, 1)
            for s in range(SLOTS):
                sp.wait_ge(landed[s], NL * UNITS // SLOTS * 16)

        @block.tensor
        def _(pe):
            mm, tr = nc.tensor.matmul, nc.tensor.transpose

            pe.sem_inc(S["ada_feat"], CREDIT["ada_feat"])
            pe.sem_inc(unit_done, SLOTS)
            pe.wait_ge(set_pool, 2)
            pe.wait_ge(set_load[1], 32)
            for t in range(2):
                for k in range(KT):
                    last = tr(BK[2 * t + k // 4][:, (k % 4) * P:(k % 4 + 1) * P],
                              stage[:, t, k * P:(k + 1) * P], ident[:, :])
            last.then_inc(set_pe, 1)
            pe.wait_ge(set_load[2], 48)
            pe.wait_ge(set_dve, 1)
            for k in range(KT):
                tr(BK[0][:, k * 8:k * 8 + 8], xc[0:8, 0, k * P:(k + 1) * P], ident[0:8, 0:8])
            for k in range(KT):
                last = tr(BK[1][:, k * 9:k * 9 + 9], xc[0:9, 1, k * P:(k + 1) * P], ident[0:9, 0:9])
            last.then_inc(set_pe, 1)
            pe.wait_ge(set_load[0], 16 * N_ROWS)
            for j in range(NL):
                tr(AUX[0][:, j * 76:(j + 1) * 76], rows[0:76, j, :], ident[0:76, 0:76])
            for j in range(NL):
                last = tr(AUX[1][:, j * 72:(j + 1) * 72], rows[0:72, 2 + j, :], ident[0:72, 0:72])
            last.then_inc(set_pe, 1)
            pe.wait_ge(set_pool, 6)
            pe.wait_ge(set_dve, 3)

            def ada_part(L, q, slot, ps, s):
                for k in range(2):
                    kt = s * 2 + k
                    for w in (whi, wlo):
                        last = mm(ps[:, :], cst[:, kt], w[:, slot, k * 512:(k + 1) * 512],
                                  start=(kt == 0 and w is whi), stop=(kt == KT - 1 and w is wlo))
                last.then_inc(unit_done, 1)

            def features(ps, par_):
                for j in range(4):
                    last = mm(ps[:, j * 9:j * 9 + 9], ada_row[:, par_, j * P:(j + 1) * P], sel[:, :],
                              start=True, stop=True)
                last.then_inc(S["ada_feat"], 1)

            def to_features(L, n, par_):
                wait(pe, "ada_row", L, n)
                wait(pe, "mod_ready", L, n - 1)
                features(AUX[2], par_)

            def sum_squares(L, sub):
                for k in range(KT):
                    last = add_squares(L, sub, k)
                return last

            def add_squares(L, sub, k):
                wait(pe, "sq_ready", L, (sub - 1) * KT + k)
                return mm(AUX[3][:, 0:NT], ones[:, 0:P], tmp[:, k], start=(k == 0), stop=(k == KT - 1))

            def keep_warm(n):
                for _ in range(n):
                    mm(AUX[1][:, 0:T], ones[:, 0:P], ones[:, :], start=True, stop=True)

            def ada0(L):
                q0 = BASE["ada0"] // SLOTS

                def chunk(c, par_):
                    for s in range(SLOTS):
                        unit_ready(pe, L, q0 + c, s)
                        if s == 0 and not (isinstance(c, int) and c < 2):
                            wait(pe, "ada_row", L, c - 2)
                        ada_part(L, q0 + c, s, AUX[par_], s)

                sum_squares(L, 0).then_inc(S["ms_done"], 1)
                chunk(0, 0)
                settle(pe)
                with pe.Fori(0, (NADA - 2) // 2) as i:
                    chunk(i * 2 + 1, 1)
                    to_features(L, i * 2, 0)
                    chunk(i * 2 + 2, 0)
                    to_features(L, i * 2 + 1, 1)
                chunk(NADA - 1, 1)
                to_features(L, NADA - 2, 0)

            def ffn(L, f):
                with pe.Fori(0, FT // 2) as i:
                    for s in range(SLOTS):
                        q = BASE[f"in{f}"] // SLOTS + i
                        unit_ready(pe, L, q, s)
                        b = G_BASE[f"in{f}"]
                        e = "AV"[s % 2]
                        n = ev_count(e, b)
                        pe.wait_ge(evac[e], L * EV_TOT[e] + (i * 2 + (n + s // 2 if n or s >= 2 else 1)))
                        for k in range(KT):
                            if s == 0 and k % 2 == 0:
                                wait(pe, "h_lo", L, f * 8 + k // 2)
                            last = mm3(BK[s][:, 0:NT], s, k * P, hH[:, k], hL[:, k], k == 0, k == KT - 1)
                        last.then_inc(unit_done, 1)
                if f == 0:
                    to_features(L, NADA - 1, 1)
                with pe.Fori(0, 2) as i:
                    for u, (kind, t, part) in enumerate(OUT_SEQ[f]):
                        q, s = out_qs(f, i, u)
                        unit_ready(pe, L, q, s)
                        if kind == "a":
                            if part == 0:
                                wait(pe, "ada_row", L, i * 3 + (NADA + t - (2 if t else 1)))
                            ada_part(L, q, s, AUX[ADA_PAR[t]], part)
                            if part == 1 and t > 0:
                                to_features(L, i * 3 + (NADA + t - 1), ADA_PAR[t - 1])
                            continue
                        if (t, part) == (0, 0):
                            wait(pe, "hid_lo", L, f * FT + 15)
                        if (t, part) == (0, 2):
                            wait(pe, "hid_lo", L, f * FT + FT - 1)
                        if part == 0:
                            for e in "AV":
                                n = ev_count(e, G_BASE[f"out{f}"]) + 1
                                pe.wait_ge(evac[e], L * EV_TOT[e] + (n if e == "A" else
                                           (n if t == 0 else n + t - 1) + i * 3))
                        for k in range(OUT_K[part]):
                            kt = part * 8 + k
                            last = mm3(BK[t][:, 0:NT], s, k * P, hidH[:, kt], hidL[:, kt],
                                       kt == 0, kt == FT - 1)
                        last.then_inc(unit_done, 1)
                    if f == 0:
                        to_features(L, i * 3 + (NADA + 2), ADA_PAR[2])

            def level(L, br, li):
                m = LEVELS[li]
                base = 0 if br == "A" else 2
                if m:
                    wait(pe, br + "_mul", L, li - 1)
                if li:
                    wait(pe, br + "_sc", L, li - 1)
                for tile in range(2):
                    if m == 128 and tile == 1:
                        continue
                    for h in range(H):
                        if br == "A":
                            sel_ = lambda t_, h=h: t_[:, h]
                        else:
                            sel_ = lambda t_, h=h: t_[64 * (h % 2):64 * (h % 2) + 64, h // 2]
                        if m == 0:
                            k_, q_ = sel_(K[br]), sel_(Q[br])
                        else:
                            k_ = q_ = sel_(X[br][:, li % 2])
                        s0 = tile * P
                        t0 = P if m == 128 else tile * P
                        bank, col = (tile, h * P) if br == "A" else (h % 2, (h // 2 * 2 + tile) * P)
                        out, q_ = AUX[base + bank][:, col:col + P], q_[:, t0:t0 + P]
                        if 0 < m < P:
                            out, q_ = (v_.rearrange("p (n two m) -> p n two m", two=2, m=m)[:, :, 1]
                                       for v_ in (out, q_))
                        last = mm(out, k_[:, s0:s0 + P], q_, start=True, stop=True)
                last.then_inc(S[br + "_mm"], 1)

            def values_T(L, br):
                base = 0 if br == "A" else 2
                for t in range(2):
                    for h in range(H):
                        last = tr(AUX[base + t][:, h * P:(h + 1) * P], V[br][:, h, t * P:(t + 1) * P], ident[:, :])
                last.then_inc(S[br + "_vT"], 1)

            def sample_T(L, n):
                src = (K["A"], V["A"], K["C"], V["C"])[n]
                if n >= 1:
                    wait(pe, "sTe", L, n - 1)
                for h in range(2 if n == 2 else 4):
                    last = tr(AUX[3][0:NB, h * P:(h + 1) * P], src[:, h, T:NT], ident[:, :])
                last.then_inc(S["sT"], 1)

            def outputs(L, br):
                wait(pe, br + "_sc", L, 8)
                wait(pe, br + "_vTe", L)
                for h in range(H):
                    o = AUX[h // 2][:, (h % 2) * T:(h % 2 + 1) * T]
                    v0, v1 = (VT[br][:, t, h * P:(h + 1) * P] for t in range(2))
                    mm(o, v0, sc[br][:, h, 0:T], start=True, stop=False)
                    last = mm(o[:, P:T], v1, sc[br][:, h, T:T + P], start=False, stop=True)
                last.then_inc(S[br + "_o"], 1)

            def kend_T(L, br):
                wait(pe, br + "_kend", L)
                for t in range(2):
                    for h in range(4 if br == "A" else 2):
                        last = tr(AUX[2 + t][:, h * P:(h + 1) * P], X[br][:, 1, h, t * P:(t + 1) * P], ident[:, :])
                last.then_inc(S[br + "_kT"], 1)

            def final_state(L, br):
                wait(pe, br + "_kTe", L)
                dk = P if br == "A" else 64
                for h in range(H):
                    for t in range(2):
                        last = mm(AUX[2][0:dk, h * P:(h + 1) * P], KTT[:, t, h * dk:(h + 1) * dk],
                                  VT[br][:, t, h * P:(h + 1) * P], start=(t == 0), stop=(t == 1))
                last.then_inc(S[br + "_S"], 1)

            def sample_kv(L, i):
                br, j = BATCHES[i]
                wait(pe, "sTe", L, 3)
                if i == 0:
                    wait(pe, "A_oe", L)
                if i == 4:
                    wait(pe, "C_oe", L)
                if i not in (0, 4):
                    wait(pe, "st_new", L, i - 1)
                for e in range(1 if br == "A" else 2):
                    n = j if br == "A" else 4 + 2 * (j) + e
                    wait(pe, "vblk", L, n)
                    r0 = 0 if br == "A" else 32
                    vb = vblk[n % 2][r0:r0 + NB]
                    for half in range(2):
                        if br == "A":
                            out, kk = AUX[half][:, :], sTs[0:NB, 0, j * P:(j + 1) * P]
                        else:
                            out = AUX[half][64 * e:64 * e + 64, :]
                            kk = sTs[32:32 + NB, 0, j * P + 64 * e:j * P + 64 * e + 64]
                        last = mm(out, kk, vb[:, half * 512:(half + 1) * 512], start=True, stop=True)
                last.then_inc(S["kv"], 1)

            def sample_o(L, i):
                br, j = BATCHES[i]
                wait(pe, "st_new", L, i)
                if i == 0:
                    wait(pe, "A_kTe", L)
                if i == 4:
                    wait(pe, "C_kTe", L)
                    wait(pe, "C_Se", L)
                for e in range(1 if br == "A" else 2):
                    for b in range(NB):
                        if br == "A":
                            w, q_, h = st[:, i % 2, b], Q["A"][:, j, T + b:T + b + 1], j
                        else:
                            r = slice(64 * e, 64 * e + 64)
                            w, q_, h = st[r, i % 2, b], Q["C"][r, j, T + b:T + b + 1], 2 * j + e
                        bank = 3 if br == "A" or e == 0 else 2
                        last = mm(AUX[bank][:, h * NB + b:h * NB + b + 1], w, q_, start=True, stop=True)
                last.then_inc(S["so"], 1)

            def head_ms(L, br):
                wait(pe, br + "_sq", L)
                wait(pe, br + "_Se", L)
                for h in range(H):
                    last = mm(AUX[0][0:H, 0:NT], onecol[:, H - 1 - h:2 * H - 1 - h], X["A"][:, 0, h],
                              start=(h == 0), stop=(h == H - 1))
                last.then_inc(S[br + "_ms"], 1)

            def head_spread(L, br):
                wait(pe, br + "_rec", L)
                for h in range(H):
                    last = mm(AUX[h][:, 0:NT], bc(ident[0:H, h:h + 1], [H, P]), X["A"][0:H, 1, 0], start=True, stop=True)
                last.then_inc(S[br + "_spread"], 1)

            def mixer(L):
                g = [0]

                def take_bank():
                    bank_free(pe, L, "mix", g[0])
                    g[0] += 1
                    return BK[(g[0] - 1) % 4][:, 0:NT]

                pe.wait_ge(rows_in, (L + 1) * 32)
                settle(pe)
                for j in range(4):
                    tr(AUX[0][:, j * 32:j * 32 + 24], crow[:, j * P:(j + 1) * P], ident[0:24, 0:24])
                    last = tr(AUX[0][:, j * 32 + 24:j * 32 + 32], hrow[:, j * P:(j + 1) * P], ident[0:8, 0:8])
                last.then_inc(S["rowsT"], 1)
                for u, (kind, what, j) in enumerate(MIX):
                    q, s = mix_qs(u)
                    unit_ready(pe, L, q, s)
                    if kind == "ada":
                        if j == 0:
                            bank_free(pe, L, "mix", g[0])
                            g[0] += 1
                            ada_ps = BK[(g[0] - 1) % 4]
                        ada_part(L, q, s, ada_ps, j)
                    elif kind == "in":
                        ps = take_bank()
                        for k in range(KT):
                            if u == 0 and k % 2 == 0:
                                wait(pe, "h_lo", L, 4 + k // 2)
                            last = mm3(ps, s, k * P, hH[:, k], hL[:, k], k == 0, k == KT - 1)
                    elif kind == "ca":
                        if j == 0:
                            ps = take_bank()
                        for k in range(4):
                            last = mm3(ps, s, k * P, hH[:, 4 * j + k], hL[:, 4 * j + k],
                                       k + j == 0, (k, j) == (3, 1))
                    elif kind == "rg":
                        wait(pe, "conv_lo", L)
                        for n in range(4):
                            last = mm3(take_bank(), s, n * P, yH[:, 8 + n], yL[:, 8 + n], True, True)
                    elif kind == "br":
                        y0 = {"a": 0, "b": 4, "c": 8}[what]
                        wait(pe, {"a": "A_lo", "b": "yb_lo", "c": "C_lo"}[what], L)
                        for n in range(2):
                            ps = take_bank()
                            for k in range(4):
                                last = mm3(ps, s, k * 256 + n * P, yH[:, y0 + k], yL[:, y0 + k], k == 0, k == 3)
                    else:
                        ps = take_bank()
                        for k in range(KT):
                            if j == 0:
                                wait(pe, "m_lo", L, k)
                            last = mm3(ps, s, k * P, yH[:, k], yL[:, k], k == 0, k == KT - 1)
                    if kind != "ada":
                        last.then_inc(unit_done, 1)
                    for n, (e, w, c, ug) in enumerate(MG):
                        if ug == u and w == "adaf":
                            evacuated(pe, L, "ada", c)
                            ps = take_bank()
                            features(ps, c % 2)
                    if what == "o" and j >= 2:
                        add_squares(L, 2, j - 2)
                    place, u = u, OLD[u]
                    if u == 13:
                        wait(pe, "rows_evac", L)
                        evacuated(pe, L, "i", 3)
                        values_T(L, "A")
                    if u == 14:
                        evacuated(pe, L, "ca", 0)
                        pe.wait_ge(wal_in, (L + 1) * 16)
                        for jj in range(2):
                            last = mm(AUX[2][:, jj * 256:jj * 256 + 256], wal[:, jj * P:(jj + 1) * P],
                                      ca[:, 0:256], start=True, stop=True)
                        for jj in range(2):
                            last = mm(AUX[3][:, jj * 8:jj * 8 + 8], wal[:, jj * P:(jj + 1) * P],
                                      ca[:, 256:264], start=True, stop=True)
                        last.then_inc(S["C_alpha"], 1)
                    if u == 15:
                        wait(pe, "A_kk", L)
                        wait(pe, "C_z", L)
                        sample_T(L, 0)
                    if u == 16:
                        wait(pe, "A_vTe", L)
                        sample_T(L, 1)
                    if u == 18:
                        evacuated(pe, L, "ck", 1)
                        sample_T(L, 2)
                    if u == 22:
                        evacuated(pe, L, "cv", 3)
                        sample_T(L, 3)
                    if u == 23:
                        wait(pe, "sTe", L, 3)
                        values_T(L, "C")
                    for li in range(9):
                        if u == PE_LV["A"][li]:
                            level(L, "A", li)
                        if u == PE_LV["C"][li]:
                            if li == 0:
                                wait(pe, "C_vTe", L)
                                wait(pe, "C_cum", L)
                            level(L, "C", li)
                    if u == 53:
                        wait(pe, "C_sc", L, 8)
                        outputs(L, "A")
                        kend_T(L, "A")
                    if u == 54:
                        final_state(L, "A")
                    if 55 <= u < 59:
                        sample_o(L, u - 55)
                    if 54 <= u < 58:
                        sample_kv(L, u - 54)
                    for br, uu in (("A", 59), ("C", 65)):
                        if place == at(uu, HEAD["ms"]):
                            head_ms(L, br)
                        if place == at(uu, HEAD["spread"]):
                            head_spread(L, br)
                    if u == 61:
                        wait(pe, "A_y", L)
                        outputs(L, "C")
                        kend_T(L, "C")
                    if u == 62:
                        final_state(L, "C")
                    if 63 <= u < 65:
                        sample_o(L, u - 59)
                    if 62 <= u < 64:
                        sample_kv(L, u - 58)
                    if u == 68:
                        wait(pe, "C_y", L)
                        for jj in range(4):
                            last = tr(AUX[0][0:20, jj * P:(jj + 1) * P], tail[:, jj], ident[:, :])
                        last.then_inc(S["tailT"], 1)
                add_squares(L, 2, KT - 2)
                add_squares(L, 2, KT - 1).then_inc(S["ms_done"], 1)

            with pe.Fori(0, NL) as L:
                ada0(L)
                ffn(L, 0)
                sum_squares(L, 1).then_inc(S["ms_done"], 1)
                keep_warm(WARM)
                mixer(L)
                keep_warm(WARM)
                ffn(L, 1)

            sum_squares(NL, 0).then_inc(fin_pe, 1)
            pe.wait_ge(fin_dve, 1)
            for t in range(2):
                for k in range(KT):
                    last = tr(BK[2 * t + k // 4][:, (k % 4) * P:(k % 4 + 1) * P], tmp[:, k, t * P:(t + 1) * P],
                              ident[:, :])
            last.then_inc(fin_pe, 1)
            for k in range(KT):
                last = tr(BK[4 + k // 4][0:NB, (k % 4) * P:(k % 4 + 1) * P], tmp[:, k, T:NT], ident[:, :])
            last.then_inc(fin_pe, 1)

        def level_views(br, li):
            m = LEVELS[li]
            r = lambda t_: t_.rearrange("p h (n two m) -> p h n two m", two=2, m=m)
            b = r(B[br][:, :, 0:T])
            e = r(X[br][:, li % 2, :, 0:T])
            shape = [P, 4 if br == "A" else 2, T // (2 * m), m]
            ref = bc(b[:, :, :, 0, m - 1:m], shape)
            return m, r, b, e, ref

        @block.gpsimd
        def _(pool):
            g = nc.gpsimd
            g.memset(ident[:, :], 0.0).then_inc(set_pool, 1)
            pool.wait_ge(set_pool, 1)
            g.affine_select(out=ident[:, :], in_=ident[:, :], compare_op=ALU.not_equal, fill=1.0, base=0,
                            pattern=[[-1, P]], channel_multiplier=1).then_inc(set_pool, 1)
            g.memset(sel[:, :], 0.0).then_inc(set_pool, 1)
            pool.wait_ge(set_pool, 3)
            for n, base in enumerate((0, -32)):
                g.affine_select(out=sel[:, :], in_=sel[:, :], compare_op=ALU.not_equal, fill=1.0, base=base,
                                pattern=[[-1, 9]], channel_multiplier=1).then_inc(set_pool, 1)
                pool.wait_ge(set_pool, 4 + n)
            g.memset(onecol[:, :], 0.0).then_inc(set_onecol, 1)
            pool.wait_ge(set_onecol, 1)
            g.memset(onecol[:, H - 1:H], 1.0)
            g.memset(ones[:, :], 1.0)
            g.memset(epst[:, :], EPS)
            g.memset(cst[:, :, :].bitcast(F), 0.0)
            for br in "AC":
                g.memset(sc[br][:, :, :], 0.0)
            g.iota(mask[:, 0, :].bitcast(I32), pattern=[[1, P]], base=0, channel_multiplier=0)
            g.iota(mask[:, 1, :].bitcast(I32), pattern=[[0, P]], base=0, channel_multiplier=1)\
             .then_inc(set_pool, 1)
            pool.wait_ge(set_pool, 6)
            n_mask = [1]

            def pm_(ins):
                ins.then_inc(set_mask, 1)
                n_mask[0] += 1
                pool.wait_ge(set_mask, n_mask[0])

            pool.wait_ge(set_mask, 1)
            pm_(g.tensor_tensor(mask[:, 0, :], mask[:, 4, :], mask[:, 3, :], ALU.mult))
            for k in range(7, 0, -1):
                pm_(g.tensor_single_scalar(mask[:, k, :], mask[:, 0, :], float(2 ** (k - 1)), ALU.is_ge))
            for k in range(1, 7):
                pm_(g.tensor_tensor(mask[:, k, :], mask[:, k, :], mask[:, k + 1, :], ALU.subtract))
            pm_(g.tensor_copy(mask[:, 0, :], ident[:, :]))

            def args(L, br, li):
                m, r, b, e, ref = level_views(br, li)
                if li >= 3:
                    wait(pool, br + "_mm", L, li - 2)
                g.tensor_tensor(e[:, :, :, 1], b[:, :, :, 1], ref, ALU.subtract)
                g.tensor_tensor(e[:, :, :, 0], ref, b[:, :, :, 0], ALU.subtract).then_inc(S[br + "_arg"], 1)

            def kend_args(L, br):
                wait(pool, br + "_mm", L, 7)
                n = 4 if br == "A" else 2
                g.tensor_tensor(X[br][:, 1, :, 0:T], bc(B[br][:, :, T - 1:T], [P, n, T]), B[br][:, :, 0:T],
                                ALU.subtract).then_inc(S[br + "_kearg"], 1)

            def st_load(L, i):
                br, j = BATCHES[i]
                if i >= 2:
                    wait(pool, "so", L, i - 2)
                    pool.wait_ge(st_out[i % 2], L * 48 + (i // 2) * 16)
                if br == "A":
                    src = state_hgrn[bass.ds(L, 1), :, j].rearrange("o b d v -> d (o b) v")
                    settle(pool)
                    g.dma_start(st[:, i % 2], src).then_inc(st_in[i % 2], 16)
                else:
                    src = state_gla[bass.ds(L, 1), :, 2 * j:2 * j + 2].rearrange("o b e d v -> e d (o b) v")
                    for e in range(2):
                        settle(pool)
                        g.dma_start(st[64 * e:64 * e + 64, i % 2], src[e]).then_inc(st_in[i % 2], 16)

            def st_store(L, i):
                br, j = BATCHES[i]
                wait(pool, "st_new", L, i)
                if br == "A":
                    dst = hg_s[bass.ds(L, 1), :, j].rearrange("o b d v -> d (o b) v")
                else:
                    dst = gl_s[bass.ds(L, 1), :, 2 * j:2 * j + 2].rearrange("o b e d v -> (e d) (o b) v")
                settle(pool)
                g.dma_start(dst, st[:, i % 2]).then_inc(st_out[i % 2], 16)

            def v_blocks(L, n):
                r0, h = (0, n) if n < 4 else (32, n - 4)
                if n == 0:
                    wait(pool, "sTe", L, 3)
                    wait(pool, "A_kearg", L)
                if n >= 2:
                    wait(pool, "kv", L, {2: 0, 3: 1, 4: 2, 5: 3, 6: 4, 7: 4}[n])
                g.tensor_tensor(vblk[n % 2][r0:r0 + NB].rearrange("p (b v) -> p b v", b=NB),
                                bc(sTs[r0:r0 + NB, 1:2, h * P:(h + 1) * P], [NB, NB, P]),
                                bc(ident[r0:r0 + NB, r0:r0 + NB].rearrange("p (b o) -> p b o", o=1), [NB, NB, P]),
                                ALU.mult).then_inc(S["vblk"], 1)

            def mixer(L):
                lx = bass.ds(L, 1)
                wait(pool, "x_ready", L, KT - 1)
                settle(pool)
                g.dma_start(crow[:, 0:512], state_conv[lx].rearrange("o b j d -> (o b j) d")).then_inc(rows_in, 16)
                settle(pool)
                g.dma_start(hrow[:, 0:512], state_rglru[lx].rearrange("o b d -> (o b) d")).then_inc(rows_in, 16)
                settle(pool)
                g.dma_start(wal[:, :], gla_w_alpha[lx].rearrange("o r n -> (o r) n")).then_inc(wal_in, 16)
                settle(pool)
                g.dma_start(cv_s[lx, :, 0:2].rearrange("o b j d -> (o b) (j d)"),
                            state_conv[lx, :, 1:3].rearrange("o b j d -> (o b) (j d)")).then_inc(direct, 16)
                st_load(L, 0)
                st_load(L, 1)
                wait(pool, "A_cum", L)
                order = sorted([(p, br, li) for br in "AC" for li, p in enumerate(PE_LV[br]) if li])
                for n, (p, br, li) in enumerate(order):
                    if br == "C" and li == 1:
                        wait(pool, "C_cum", L)
                    args(L, br, li)
                kend_args(L, "A")
                kend_args(L, "C")
                for i in range(6):
                    if i < 4:
                        v_blocks(L, i)
                    else:
                        v_blocks(L, 2 * i - 4)
                        v_blocks(L, 2 * i - 3)
                    if i >= 1:
                        st_store(L, i - 1)
                    if 1 <= i < 5:
                        st_load(L, i + 1)
                    if i == 2:
                        wait(pool, "A_Se", L)
                        settle(pool)
                        g.dma_start(hg_p[lx, 0].rearrange("o h d v -> d (o h) v"), stF[:, :, :])\
                         .then_inc(fin_out, 16)
                st_store(L, 5)
                wait(pool, "C_Se", L)
                settle(pool)
                g.dma_start(gl_p[lx, 0].rearrange("o h d v -> d (o h) v"), stF[0:64, :, :]).then_inc(fin_out, 16)
                wait(pool, "tail_evac", L)
                settle(pool)
                g.dma_start(cv_p[lx, 0].rearrange("o j d -> (o j) d"), crow[0:3, 0:512]).then_inc(stored, 16)
                settle(pool)
                g.dma_start(cv_s[lx, :, 2].rearrange("o b d -> (o b) d"), crow[3:11, 0:512]).then_inc(stored, 16)
                settle(pool)
                g.dma_start(rl_p[lx, 0], crow[11:12, 0:512]).then_inc(stored, 16)
                settle(pool)
                g.dma_start(rl_s[lx].rearrange("o b d -> (o b) d"), crow[12:20, 0:512]).then_inc(stored, 16)

            with pool.Fori(0, NL) as L:
                mixer(L)
            for i in range(2):
                pool.wait_ge(st_out[i], NL * 48)
            pool.wait_ge(fin_out, NL * 32)
            pool.wait_ge(stored, NL * 64)
            pool.wait_ge(direct, NL * 16)

        @block.scalar
        def _(act):
            def a(out, in_, func, **k):
                return nc.scalar.activation(out, in_, func, **k)

            act.sem_inc(evac["A"], 1)
            act.sem_inc(S["ada_row"], CREDIT["ada_row"])
            act.sem_inc(act_seq, 1)
            for t in range(2):
                act.dma_start(stage[:, t, :], x_prompt[0, t * P:(t + 1) * P, :]).then_inc(set_load[1], 16)
            act.dma_start(xc[0:8, 0, :], x_sample[:, 0, :]).then_inc(set_load[2], 16)
            act.dma_start(xc[0:1, 1, :], c_prompt).then_inc(set_load[2], 16)
            act.dma_start(xc[1:9, 1, :], c_sample).then_inc(set_load[2], 16)
            for l in range(NL):
                for row, src in row_src[l]:
                    act.dma_start(rows[row:row + src.shape[0], l, :], src).then_inc(set_load[0], 16)
                act.dma_start(rows[0:72, 2 + l, :], b_ada[l].rearrange("(t p) -> t p", p=P)).then_inc(set_load[0], 16)
            for k in range(KT):
                if k == 0:
                    wait(act, "x_ready", 0, -1)
                a(tmp[:, k], x[:, k], ACT.Square).then_inc(S["sq_ready"], 1)
            act.wait_ge(set_dve, 4)
            a(setup_t[:, 0:2, 0:4], setup_t[:, 0:2, 0:4], ACT.Exp).then_inc(set_act, 1)
            a(setup_t[:, 4:6, 0:4], setup_t[:, 4:6, 0:4], ACT.Exp).then_inc(set_act, 1)
            act.wait_ge(set_act, 2)
            a(setup_t[:, 4:6, 0:4], setup_t[:, 4:6, 0:4], ACT.Ln, bias=1.0).then_inc(set_act, 1)
            act.wait_ge(set_dve, 5)
            a(par_all[:, :, PC["L1"]:PC["L1"] + 4], par_all[:, :, PC["L1"]:PC["L1"] + 4], ACT.Ln)
            a(par_all[:, :, PC["l1m"]:PC["l1m"] + 4], par_all[:, :, PC["l1m"]:PC["l1m"] + 4], ACT.Ln)\
                .then_inc(set_act, 1)

            seq = [0]

            def A_(ins):
                ins.then_inc(act_seq, 1)
                seq[0] += 1

            def own(L):
                act.wait_ge(act_seq, L * SEQ + (seq[0] + 1))

            def square(L, i):
                wait(act, "x_ready", L, i)
                a(tmp[:, i % KT], x[:, i % KT], ACT.Square).then_inc(S["sq_ready"], 1)

            def load_sqrt(L):
                a(scrap[:, :], epst[:, :], ACT.Sqrt)

            def root(L, sub):
                wait(act, "ms_done", L, sub)
                a(rstd[:, 0], AUX[3][:, 0:NT], ACT.Sqrt, bias=epst[:, 0:1], scale=1.0 / D)\
                    .then_inc(S["root_done"], 1)

            def apply_norm(L, sub, before=lambda p_: None):
                def high(p_):
                    wait(act, "h_p", L, sub * 4 + p_)
                    if p_ == 0:
                        wait(act, "h_s", L, sub)
                    a(hH[:, 2 * p_:2 * p_ + 2], tmp[:, 2 * p_:2 * p_ + 2], ACT.Copy).then_inc(S["h_hi"], 1)

                for p_ in range(4):
                    before(p_)
                    if p_ == 0:
                        wait(act, "G_ready", L, sub)
                    wait(act, "xn_ready", L, sub * 4 + p_)
                    for k in range(2 * p_, 2 * p_ + 2):
                        last = a(tmp[:, k, 0:T], tmp[:, k, 0:T], ACT.Identity, scale=Gs[:, k, 0:1],
                                 bias=mod[:, sub * 24 + k, 0:1])
                    last.then_inc(S["h_p"], 1)
                    if p_ >= 1:
                        high(p_ - 1)
                high(3)

            def ada0(L):
                q0 = BASE["ada0"] // SLOTS

                def row0(c, par_):
                    unit_used(act, L, c + q0, SLOTS - 1)
                    wait(act, "ada_feat", L, c - 2)
                    a(ada_row[:, par_], AUX[par_][0:64, :], ACT.Copy).then_inc(S["ada_row"], 1)

                for s in range(SLOTS):
                    split_hi(act, L, q0, s)
                root(L, 0)
                for s in range(SLOTS):
                    split_hi(act, L, q0 + 1, s)
                row0(0, 0)
                for s in range(SLOTS):
                    split_hi(act, L, q0 + 2, s)
                row0(1, 1)
                with act.Fori(0, (NADA - 4) // 2) as i:
                    for s in range(SLOTS):
                        split_hi(act, L, i * 2 + (q0 + 3), s)
                    row0(i * 2 + 2, 0)
                    for s in range(SLOTS):
                        split_hi(act, L, i * 2 + (q0 + 4), s)
                    row0(i * 2 + 3, 1)
                apply_norm(L, 0, lambda s: split_hi(act, L, q0 + NADA - 1, s))
                row0(NADA - 2, 0)
                for s in range(LOOK):
                    split_hi(act, L, BASE["in0"] // SLOTS, s)
                row0(NADA - 1, 1)

            def ffn(L, f):
                qi, qo = BASE[f"in{f}"] // SLOTS, BASE[f"out{f}"] // SLOTS
                b = G_BASE[f"in{f}"]

                def step(i, s, ahead):
                    pair = i * 2 + s // 2
                    if s % 2 == 0:
                        unit_used(act, L, i + qi, s)
                        a(sil[:, s // 2], BK[s][:, 0:NT], ACT.Silu).then_inc(evac["A"], 1)
                        ahead()
                    else:
                        ahead()
                        act.wait_ge(evac["V"], L * EV_TOT["V"] + (pair + (ev_count("V", b) + 2)))
                        a(hidH[:, bass.ds(pair, 1)].rearrange("p o t -> p (o t)")
                          if not isinstance(pair, int) else hidH[:, pair],
                          hid[:, s // 2], ACT.Copy).then_inc(S["hid_hi"], 1)

                if f == 1:
                    act.wait_ge(stored, (L + 1) * 64)
                    act.wait_ge(fin_out, (L + 1) * 32)
                a(scrap[:, :], epst[:, :], ACT.Silu)
                with act.Fori(0, FT // 2 - 1) as i:
                    for s in range(SLOTS):
                        step(i, s, lambda: split_hi(act, L, i + (qi + (s + 3) // 4), (s + 3) % 4))
                step(FT // 2 - 1, 0, lambda: split_hi(act, L, qi + FT // 2 - 1, 3))
                for s in range(1, SLOTS):
                    step(FT // 2 - 1, s, lambda: split_hi(act, L, qo, s - 1, out_cols(f, s - 1)))
                load_sqrt(L)
                for k in range(U_OUT[f]):
                    if k + LOOK < U_OUT[f]:
                        split_hi(act, L, *out_qs(f, 0, k + LOOK), out_cols(f, k + LOOK))
                    elif f == 0:
                        mix_hi(act, L, k + LOOK - U_OUT[f])
                    i, (kind, t, part) = k // len(OUT_SEQ[f]), OUT_SEQ[f][k % len(OUT_SEQ[f])]
                    if kind == "a" and part == 3:
                        unit_used(act, L, *out_qs(f, 0, k))
                        wait(act, "ada_feat", L, NADA + i * 3 + t - (2 if t else 1))
                        a(ada_row[:, ADA_PAR[t]], AUX[ADA_PAR[t]][0:64, :], ACT.Copy).then_inc(S["ada_row"], 1)
                    if kind == "o" and part == 2 and i * 4 + t > 0:
                        square(L, 2 * f * KT + i * 4 + t - 1)
                square(L, 2 * f * KT + KT - 1)
                if f == 0:
                    root(L, 1)
                    apply_norm(L, 1)

            def mixer(L):
                z, x0, x1, kk = B["A"], X["A"][:, 0], X["A"][:, 1], K["A"]
                EVAC = {
                    "f": (ACT.Copy, lambda j: B["A"][:, j]), 
                    "bx": (ACT.Copy, lambda j: XB[:, j]), "bg": (ACT.Gelu_apprx_tanh, lambda j: XB[:, 4 + j]),
                    "wa": (ACT.Tanh, lambda j: tmp[:, 4 + j]), "wx": (ACT.Tanh, lambda j: XB[:, j]),
                    "ma": (ACT.Tanh, lambda j: XB[:, j]), "mb": (ACT.Tanh, lambda j: sg[:, j % 2]),
                    "mc": (ACT.Tanh, lambda j: sg[:, j % 2]),
                }
                for u, (kind, what, j) in enumerate(MIX):
                    if u + LOOK < U_MIX:
                        mix_hi(act, L, u + LOOK)
                    else:
                        split_hi(act, L, BASE["in1"] // SLOTS, u + LOOK - U_MIX)
                    for n, (e, w, t, ug) in enumerate(MG):
                        if ug != u or e != "A":
                            continue
                        unit_used(act, L, *mix_qs(u))
                        if w == "ada":
                            wait(act, "ada_feat", L, 2 * NADA + t - 2)
                            a(ada_row[:, t % 2], BK[n % 4][0:64, :], ACT.Copy).then_inc(evac["A"], 1)
                            continue
                        if w == "wx" or w == "wa":
                            wait(act, "conv_lo", L)
                        if w == "ma":
                            wait(act, "yb_lo", L)
                        if w == "mb" and t >= 2:
                            evacuated(act, L, "brb", t - 2)
                        if w == "mc" and t < 2:
                            evacuated(act, L, "brb", 6 + t)
                        if w == "mc" and t >= 2:
                            evacuated(act, L, "brc", t - 2)
                        fn, dst = EVAC[w]
                        kw = dict(scale=0.5) if fn == ACT.Tanh else {}
                        if w in ("wa", "wx"):
                            c = PC["rba" if w == "wa" else "rbx"] + t
                            kw["bias"] = par[:, c:c + 1]
                        if w == "bx":
                            a(tmp[:, t], BK[n % 4][:, 0:NT], ACT.Identity, scale=par[:, PC["convw"] + 12 + t:PC["convw"] + 13 + t],
                              bias=par[:, PC["convb"] + t:PC["convb"] + t + 1])
                        a(dst(t), BK[n % 4][:, 0:NT], fn, **kw).then_inc(evac["A"], 1)
                    if what in ("q", "cg", "ag"):
                        unit_used(act, L, *mix_qs(u))
                        if what == "ag":
                            wait(act, "rg_u", L)
                        dst = Q["A"] if what == "q" else GT[what[0].upper()]
                        a(dst[:, j], BK[GI[(what, j)] % 4][:, 0:NT], ACT.Tanh, scale=0.5)\
                            .then_inc(S["g_tanh"], 1)
                    place, u = u, OLD[u]
                    if u == 5:
                        wait(act, "A_abs", L)
                        A_(a(x1, x1, ACT.Exp))
                        own(L)
                        a(x1, x1, ACT.Ln, bias=1.0).then_inc(S["A_ln"], 1)
                    if u == 7:
                        wait(act, "A_ls", L)
                        a(kk[:, :, :], kk[:, :, :], ACT.Exp).then_inc(S["A_k"], 1)
                    if u == 9:
                        wait(act, "A_diff", L)
                        A_(a(x1, x1, ACT.Exp))
                        own(L)
                        a(x1, x1, ACT.Ln, bias=1.0).then_inc(S["A_ln2"], 1)
                    if u == 11:
                        wait(act, "A_logf", L)
                        a(fS[:, 0:4, :], z[:, :, T:NT], ACT.Exp).then_inc(S["A_fS"], 1)
                    if u == 14:
                        wait(act, "A_vT", L)
                        for t in range(2):
                            last = a(VT["A"][:, t], AUX[t][:, :], ACT.Copy)
                        last.then_inc(S["A_vTe"], 1)
                    if u == 16:
                        c1_ = X["C"][:, 1]
                        wait(act, "C_abs", L)
                        A_(a(c1_, c1_, ACT.Exp))
                        own(L)
                        a(c1_, c1_, ACT.Ln, bias=1.0).then_inc(S["C_ln"], 1)
                    if u == 18:
                        wait(act, "C_logf", L)
                        a(fS[:, 4:6, :], B["C"][:, :, T:NT], ACT.Exp).then_inc(S["C_fS"], 1)
                    if u == 24:
                        wait(act, "C_vT", L)
                        for t in range(2):
                            last = a(VT["C"][:, t], AUX[2 + t][:, :], ACT.Copy)
                        last.then_inc(S["C_vTe"], 1)
                    for br in "AC":
                        for li in range(1, 9):
                            if u == PE_LV[br][li] - 3:
                                wait(act, br + "_arg", L, li - 1)
                                e = X[br][:, li % 2, :, 0:T]
                                a(e, e, ACT.Exp).then_inc(S[br + "_exp"], 1)
                        if u == (50 if br == "A" else 51):
                            wait(act, br + "_kearg", L)
                            e = X[br][:, 1, :, 0:T]
                            a(e, e, ACT.Exp).then_inc(S[br + "_keexp"], 1)
                    if u == 28:
                        wait(act, "conv", L)
                        a(yH[:, 8:12], tmp[:, 0:4], ACT.Copy).then_inc(S["conv_hi"], 1)
                    if u == 32:
                        wait(act, "rg_arg", L)
                        a(GT["A"][:, :], tmp[:, 4:8], ACT.Tanh)
                        a(tmp[:, 4:8], tmp[:, 4:8], ACT.Exp, scale=2.0).then_inc(S["rg_tanh"], 1)
                    if u == 34:
                        wait(act, "rg_nt", L)
                        a(GT["A"][:, :], GT["A"][:, :], ACT.Sqrt).then_inc(S["rg_sqrt"], 1)
                    if u == 38:
                        wait(act, "yb", L)
                        a(yH[:, 4:8], XB[:, 4:8], ACT.Copy).then_inc(S["yb_hi"], 1)
                    O_SCALE = {"A": 0.5, "C": 1.0}
                    for br, u0 in (("A", 54), ("C", 62)):
                        if u == u0:
                            wait(act, br + "_o", L)
                            for t in range(2):
                                last = a(O[br][:, 2 * t:2 * t + 2, 0:T],
                                         AUX[t][:, :].rearrange("p (h t) -> p h t", h=2), ACT.Copy,
                                         scale=O_SCALE[br])
                            last.then_inc(S[br + "_oe"], 1)
                        if u == u0 + 1:
                            wait(act, br + "_S", L)
                            dk = P if br == "A" else 64
                            if br == "C":
                                act.wait_ge(fin_out, L * 32 + 16)
                            a(stF[0:dk], AUX[2][0:dk, :].rearrange("p (h v) -> p h v", h=4), ACT.Copy)\
                                .then_inc(S[br + "_Se"], 1)
                    for br, u0, y0 in (("A", 59, 0), ("C", 65, 8)):
                        if place == at(u0):
                            wait(act, "so", L, 3 if br == "A" else 5)
                            if br == "A":
                                A_(a(O[br][:, :, T:NT], AUX[3][:, 0:32].rearrange("p (h b) -> p h b", h=4), ACT.Copy,
                                     scale=O_SCALE[br]))
                            else:
                                for e in range(2):
                                    A_(a(O[br][:, :, T:NT].rearrange("p (j e) b -> p j e b", e=2)[:, :, e],
                                         AUX[3 - e][:, 0:32].rearrange("p (j e b) -> p j e b", j=2, e=2)[:, :, e],
                                         ACT.Copy))
                            load_sqrt(L)
                            own(L)
                            if br == "C":
                                wait(act, "A_lo", L)
                            wait(act, br + "_kTe", L)
                            a(X["A"][:, 0], O[br][:, :, :], ACT.Square).then_inc(S[br + "_sq"], 1)
                        if place == at(u0, HEAD["root"]):
                            wait(act, br + "_ms", L)
                            a(X["A"][0:H, 1, 0], AUX[0][0:H, 0:NT], ACT.Sqrt, bias=epst[0:H, 0:1],
                              scale=1.0 / P).then_inc(S[br + "_root"], 1)
                        if place == at(u0, HEAD["high"]):
                            wait(act, br + "_y", L)
                            a(yH[:, y0:y0 + 4], O[br][:, :, :], ACT.Copy).then_inc(S[br + "_hi"], 1)
                    if what == "o" and j > 0:
                        square(L, KT + j - 1)
                    if kind == "br" and what == "c":
                        for n in range(2 * j, 2 * j + 2):
                            wait(act, "mrg", L, n)
                            a(yH[:, n], tmp[:, n], ACT.Copy).then_inc(S["m_hi"], 1)
                load_sqrt(L)
                square(L, 2 * KT - 1)
                root(L, 2)
                apply_norm(L, 2)

            with act.Fori(0, NL) as L:
                seq[0] = 0
                ada0(L)
                ffn(L, 0)
                mixer(L)
                ffn(L, 1)
                own(L)
                act.sem_inc(act_seq, SEQ - seq[0])

            act.sem_inc(fin_act, 1)
            act.wait_ge(fin_pe, 1)
            a(rstd[:, 0], AUX[3][:, 0:NT], ACT.Sqrt, bias=epst[:, 0:1], scale=1.0 / D).then_inc(fin_act, 1)
            act.wait_ge(fin_pe, 2)
            for t in range(2):
                for half in range(2):
                    last = a(stage[:, t, half * 512:(half + 1) * 512], BK[2 * t + half][:, :], ACT.Copy)
                last.then_inc(fin_act, 1)
                act.wait_ge(fin_act, 3 + t)
                act.dma_start(y_p[0, t * P:(t + 1) * P, :], stage[:, t, :]).then_inc(y_out, 16)
            act.wait_ge(fin_dve, 2)
            act.dma_start(y_s[:, 0, :], xc[0:NB, 0, :]).then_inc(y_out, 16)
            act.wait_ge(y_out, 48)

        @block.vector
        def _(dve):
            v = nc.vector
            tt = lambda o, i0, i1, op: v.tensor_tensor(o, i0, i1, op)
            ts = lambda o, i, s1, s2, o0, o1: v.tensor_scalar(o, i, s1, s2, o0, o1)

            def neg_abs(out, in_):
                return v.scalar_tensor_tensor(out, in_, -1.0, in_, ALU.mult, ALU.min)

            dve.sem_inc(lo_done, SLOTS)
            n0 = [0]

            def st_(ins):
                ins.then_inc(dve_set, 1)
                n0[0] += 1
                dve.wait_ge(dve_set, n0[0])

            dve.wait_ge(set_pe, 1)
            for t in range(2):
                for half in range(2):
                    st_(v.tensor_copy(x[:, half * 4:half * 4 + 4, t * P:(t + 1) * P],
                                      BK[2 * t + half][:, :].rearrange("p (k c) -> p k c", k=4)))
            dve.sem_inc(set_dve, 1)
            dve.wait_ge(set_pe, 2)
            st_(v.tensor_copy(x[:, :, T:NT], BK[0][:, 0:64].rearrange("p (k c) -> p k c", k=KT)))
            dve.sem_inc(S["x_ready"], CREDIT["x_ready"])
            dve.wait_ge(set_pool, 6)
            c_ps = BK[1][:, 0:72].rearrange("p (k c) -> p k c", k=KT)
            st_(v.tensor_copy(cst[:, :, 0:9], c_ps))
            st_(tt(cst[:, :, 32:41], c_ps, cst[:, :, 0:9].bitcast(F), ALU.subtract))
            dve.sem_inc(S["mod_ready"], CREDIT["mod_ready"])
            dve.sem_inc(evac["V"], 1)
            dve.sem_inc(dve_seq, 1)
            dve.sem_inc(set_dve, 1)
            dve.wait_ge(set_pe, 3)
            st_(v.tensor_copy(par_all[:, :, 0:76], AUX[0][:, 0:152].rearrange("p (l n) -> p l n", l=2)))
            st_(v.tensor_copy(par_all[:, :, 76:148], AUX[1][:, 0:144].rearrange("p (l n) -> p l n", l=2)))
            for c in (slice(PC["rba"], PC["rbx"] + 4), slice(PC["hnorm"], PC["gnorm"] + 1)):
                st_(v.tensor_single_scalar(par_all[:, :, c], par_all[:, :, c], 0.5, ALU.mult))
            dve.sem_inc(set_dve, 1)
            both = lambda n: par_all[:, :, PC[n]:PC[n] + 4]
            s4 = lambda k: setup_t[:, k, 0:4]
            s8 = lambda k: setup_t[:, k:k + NL, 0:4]
            logits = par_all[:, 0, PC["lb"]:PC["lb"] + 4 * NL].rearrange("p (l n) -> p l n", l=NL)
            st_(tt(s4(2), logits[:, 0], logits[:, 1], ALU.max))
            st_(tt(s8(0), logits, bc(setup_t[:, 2:3, 0:4], [P, NL, 4]), ALU.subtract))
            st_(neg_abs(s8(4), both("lam")))
            dve.sem_inc(set_dve, 1)
            dve.wait_ge(set_act, 2)
            st_(tt(s4(2), s4(0), s4(1), ALU.add))
            st_(v.reciprocal(s4(2), s4(2)))
            st_(tt(s8(0), s8(0), bc(setup_t[:, 2:3, 0:4], [P, NL, 4]), ALU.mult))
            st_(tt(s4(3), s4(0), s4(1), ALU.add))
            st_(tt(s4(1), s4(3), s4(0), ALU.subtract))
            st_(tt(s4(0), s4(0), s4(0), ALU.subtract))
            st_(ts(both("oml"), s8(0), -1.0, 1.0, ALU.mult, ALU.add))
            st_(v.tensor_single_scalar(both("L1"), s8(0), 2.0 ** -60, ALU.max))
            st_(v.tensor_single_scalar(both("l1m"), both("oml"), 2.0 ** -60, ALU.max))
            dve.sem_inc(set_dve, 1)
            st_(ts(s8(6), s8(0), 0.0, -1e30, ALU.is_le, ALU.mult))
            st_(ts(both("nsp"), both("lam"), -1.0, 0.0, ALU.mult, ALU.max))
            dve.wait_ge(set_act, 3)
            st_(tt(both("nsp"), both("nsp"), s8(4), ALU.add))
            st_(v.tensor_single_scalar(both("nsp"), both("nsp"), -2.0, ALU.mult))
            mi = lambda k: mask[:, k, :].bitcast(I32)
            st_(tt(mi(2), mi(0), mi(1), ALU.bitwise_xor))
            st_(tt(mask[:, 3, :], mi(0), mi(1), ALU.is_gt))
            st_(v.tensor_copy(mask[:, 4, :], mi(2)))
            dve.sem_inc(set_mask, 1)
            dve.wait_ge(set_act, 4)
            st_(tt(both("L1"), both("L1"), s8(6), ALU.add))

            seq = [0]

            def V_(ins):
                ins.then_inc(dve_seq, 1)
                seq[0] += 1

            def own(L):
                dve.wait_ge(dve_seq, L * SEQ + (seq[0] + 1))

            def to_mod(L, n, ps=None):
                wait(dve, "ada_feat", L, n)
                t0 = n * 4
                m_ = mod[:, t0:t0 + 4] if isinstance(t0, int) else mod[:, bass.ds(t0, 4)]
                c0_ = t0 + PC["bada"]
                b_ = par[:, c0_:c0_ + 4] if isinstance(t0, int) else par[:, bass.ds(c0_, 4)]
                ps = AUX[2] if ps is None else ps
                return tt(m_, ps[:, 0:36].rearrange("p (t c) -> p t c", t=4),
                          bc(b_.rearrange("p (t o) -> p t o", o=1), [P, 4, 9]), ALU.add)

            def gains(L, sub):
                gain = par[:, PC["gain"] + sub * 8:PC["gain"] + sub * 8 + 8].rearrange("p (k o) -> p k o", o=1)
                v.scalar_tensor_tensor(Gs[:, :, :], mod[:, sub * 24 + 8:sub * 24 + 16, :], 1.0,
                                       bc(gain, [P, KT, 9]), ALU.add, ALU.mult).then_inc(S["G_ready"], 1)

            def gates(L, sub):
                V_(v.tensor_single_scalar(gate[:, :, :], mod[:, sub * 24 + 16:sub * 24 + 24, :], 0.5, ALU.mult))

            def scale_samples(L, sub):
                own(L)
                wait(dve, "G_ready", L, sub)
                V_(tt(tmp[:, :, T:NT], tmp[:, :, T:NT], Gs[:, :, 1:9], ALU.mult))
                own(L)
                tt(tmp[:, :, T:NT], tmp[:, :, T:NT], mod[:, sub * 24:sub * 24 + 8, 1:9], ALU.add)\
                    .then_inc(S["h_s"], 1)

            def normed(L, sub):
                wait(dve, "root_done", L, sub)
                V_(v.reciprocal(rstd[:, 0], rstd[:, 0]))
                own(L)
                V_(tt(tmp[:, :, T:NT], x[:, :, T:NT], bc(rstd[:, :, T:NT], [P, KT, NB]), ALU.mult))
                for p_ in range(4):
                    k = slice(2 * p_, 2 * p_ + 2)
                    tt(tmp[:, k, 0:T], x[:, k, 0:T], bc(rstd[:, :, 0:T], [P, 2, T]), ALU.mult)\
                        .then_inc(S["xn_ready"], 1)
                    if p_ == 0 and sub > 0:
                        scale_samples(L, sub)

            def low(L, sub, before=lambda p_: None):
                for p_ in range(4):
                    k = slice(2 * p_, 2 * p_ + 2)
                    before(p_)
                    wait(dve, "h_hi", L, sub * 4 + p_)
                    tt(hL[:, k], tmp[:, k], hH[:, k].bitcast(F), ALU.subtract).then_inc(S["h_lo"], 1)

            def ada0(L):
                q0 = BASE["ada0"] // SLOTS
                for s in range(SLOTS):
                    split_lo(dve, L, q0, s)
                normed(L, 0)
                for s in range(SLOTS):
                    split_lo(dve, L, q0 + 1, s)
                for c in range(2, NADA - 1):
                    for s in range(SLOTS):
                        split_lo(dve, L, q0 + c, s)
                    to_mod(L, c - 2).then_inc(S["mod_ready"], 1)
                to_mod(L, 3).then_inc(S["mod_ready"], 1)
                wait(dve, "mod_ready", L, 3)
                gains(L, 0)
                scale_samples(L, 0)
                low(L, 0, lambda s: split_lo(dve, L, q0 + NADA - 1, s))
                to_mod(L, NADA - 2).then_inc(S["mod_ready"], 1)
                for s in range(LOOK):
                    split_lo(dve, L, BASE["in0"] // SLOTS, s)

            def add_tile(L, ps, t):
                V_(tt(t8[:, t], ps[:, T:NT], gate[:, t, 1:9], ALU.mult))
                v.scalar_tensor_tensor(x[:, t, 0:T], ps[:, 0:T], gate[:, t, 0:1], x[:, t, 0:T], ALU.mult, ALU.add)\
                    .then_inc(evac["V"], 1)
                own(L)
                tt(x[:, t, T:NT], x[:, t, T:NT], t8[:, t], ALU.add).then_inc(S["x_ready"], 1)

            def ffn(L, f):
                qi, qo = BASE[f"in{f}"] // SLOTS, BASE[f"out{f}"] // SLOTS
                b = G_BASE[f"in{f}"]

                def step(i, s, ahead):
                    ahead()
                    if s % 2 == 0:
                        return
                    pair = i * 2 + s // 2
                    unit_used(dve, L, i + qi, s)
                    dve.wait_ge(evac["A"], L * EV_TOT["A"] + (pair + (ev_count("A", b) + 2)))
                    tt(hid[:, s // 2], sil[:, s // 2], BK[s][:, 0:NT], ALU.mult).then_inc(evac["V"], 1)
                    wait(dve, "hid_hi", L, pair + f * FT)
                    dst, hh = (hidL[:, pair], hidH[:, pair]) if isinstance(pair, int) else (
                        t_[:, bass.ds(pair, 1)].rearrange("p o t -> p (o t)") for t_ in (hidL, hidH))
                    tt(dst, hid[:, s // 2], hh.bitcast(F), ALU.subtract).then_inc(S["hid_lo"], 1)

                if f == 1:
                    dve.wait_ge(stored, (L + 1) * 64)
                    dve.wait_ge(fin_out, (L + 1) * 32)
                    settle(dve)
                with dve.Fori(0, FT // 2 - 1) as i:
                    for s in range(SLOTS):
                        step(i, s, lambda: split_lo(dve, L, i + (qi + (s + 3) // 4), (s + 3) % 4))
                step(FT // 2 - 1, 0, lambda: split_lo(dve, L, qi + FT // 2 - 1, 3))
                for s in range(1, SLOTS):
                    step(FT // 2 - 1, s, lambda: split_lo(dve, L, qo, s - 1, out_cols(f, s - 1)))
                if f == 0:
                    to_mod(L, NADA - 1).then_inc(S["mod_ready"], 1)
                    wait(dve, "mod_ready", L, NADA - 1)
                    gates(L, 0)
                own(L)
                for k in range(U_OUT[f]):
                    if k + LOOK < U_OUT[f]:
                        split_lo(dve, L, *out_qs(f, 0, k + LOOK), out_cols(f, k + LOOK))
                    elif f == 0:
                        mix_lo(dve, L, k + LOOK - U_OUT[f])
                    i, (kind, t, part) = k // len(OUT_SEQ[f]), OUT_SEQ[f][k % len(OUT_SEQ[f])]
                    if kind == "o" and part == 2:
                        unit_used(dve, L, *out_qs(f, 0, k))
                        add_tile(L, BK[t], i * 4 + t)
                    if f == 0 and kind == "a" and (part == 1 and t > 0):
                        to_mod(L, NADA + i * 3 + t - 1).then_inc(S["mod_ready"], 1)
                    if f == 0 and k % len(OUT_SEQ[0]) == len(OUT_SEQ[0]) - 1:
                        to_mod(L, NADA + i * 3 + 2).then_inc(S["mod_ready"], 1)
                    if f == 0 and k == len(OUT_SEQ[0]) + 19:
                        wait(dve, "mod_ready", L, NADA + 3)
                        gains(L, 1)
                if f == 0:
                    normed(L, 1)
                    low(L, 1)
                    wait(dve, "mod_ready", L, 2 * NADA - 1)
                    gates(L, 1)

            def mixer(L):
                z, x0, x1, kk = B["A"], X["A"][:, 0], X["A"][:, 1], K["A"]
                zc, c0_, c1_ = B["C"], X["C"][:, 0], X["C"][:, 1]
                cv, r4, bx, bg, t4 = tmp[:, 0:4], tmp[:, 4:8], XB[:, 0:4], XB[:, 4:8], GT["A"]
                pcol = lambda n, j=0: par[:, PC[n] + j:PC[n] + j + 1]

                def conv_tiles(lo_, hi_):
                    for d in range(1, 4):
                        own(L)
                        for j in range(lo_, hi_):
                            w = pcol("convw", (3 - d) * 4 + j)
                            V_(v.scalar_tensor_tensor(cv[:, j, d:T], bx[:, j, 0:T - d], w, cv[:, j, d:T],
                                                      ALU.mult, ALU.add))
                            buf = cbuf[:, j, 0:24].rearrange("p (b i) -> p b i", i=3)[:, :, 3 - d]
                            V_(v.scalar_tensor_tensor(cv[:, j, T:NT], buf, w, cv[:, j, T:NT],
                                                      ALU.mult, ALU.add))

                def multiply(br, li):
                    m, r, b, e, ref = level_views(br, li)
                    wait(dve, br + "_exp", L, li - 1)
                    tt(e[:, :, :, 1], e[:, :, :, 1], r(Q[br][:, :, 0:T])[:, :, :, 1], ALU.mult)
                    tt(e[:, :, :, 0], e[:, :, :, 0], r(K[br][:, :, 0:T])[:, :, :, 0], ALU.mult)\
                        .then_inc(S[br + "_mul"], 1)

                def keep(br, li):
                    m = LEVELS[li]
                    wait(dve, br + "_mm", L, li)
                    settle(dve)
                    if br == "C":
                        for e in range(2):
                            ps = AUX[2 + e][:, :].rearrange("p (j t n) -> p j t n", j=2, t=2)
                            dst = sc["C"][:, :, :].rearrange("p (j e) t -> p j e t", e=2)[:, :, e]
                            if m == 128:
                                last = v.tensor_copy(dst[:, :, P:2 * P], ps[:, :, 0])
                                continue
                            for t in range(2):
                                mk = bc(mask[:, li:li + 1, :].bitcast(I32), [P, 2, P])
                                last = v.copy_predicated(dst[:, :, 2 * P * t:2 * P * t + P], mk, ps[:, :, t])
                        last.then_inc(S["C_sc"], 1)
                        return
                    ps = lambda t: AUX[t][:, :].rearrange("p (h t) -> p h t", h=4)
                    if m == 128:
                        last = v.tensor_copy(sc[br][:, :, P:2 * P], ps(0))
                    else:
                        mk = bc(mask[:, li:li + 1, :].bitcast(I32), [P, 4, P])
                        v.copy_predicated(sc[br][:, :, 0:P], mk, ps(0))
                        last = v.copy_predicated(sc[br][:, :, 2 * P:3 * P], mk, ps(1))
                    last.then_inc(S[br + "_sc"], 1)

                for u, (kind, what, j) in enumerate(MIX):
                    if u + LOOK < U_MIX:
                        mix_lo(dve, L, u + LOOK)
                    else:
                        split_lo(dve, L, BASE["in1"] // SLOTS, u + LOOK - U_MIX)
                    for n, (e, w, t, ug) in enumerate(MG):
                        if ug != u or e != "V":
                            continue
                        if w == "adaf":
                            to_mod(L, 2 * NADA + t, BK[n % 4]).then_inc(evac["V"], 1)
                            continue
                        unit_used(dve, L, *mix_qs(u))
                        ps = BK[n % 4][:, 0:NT]
                        if w == "o":
                            own(L)
                            add_tile(L, ps, t)
                        elif w in ("bra", "brb", "brc"):
                            if w == "brb":
                                evacuated(dve, L, "mb", t)
                                v.scalar_tensor_tensor(tmp[:, t], sg[:, t % 2], 1.0, ps, ALU.add, ALU.mult)\
                                    .then_inc(evac["V"], 1)
                            else:
                                s_ = XB[:, t] if w == "bra" else sg[:, t % 2]
                                evacuated(dve, L, "ma" if w == "bra" else "mc", t)
                                own(L)
                                v.scalar_tensor_tensor(rstd[:, 0], s_, 1.0, ps, ALU.add, ALU.mult)\
                                    .then_inc(evac["V"], 1)
                                evacuated(dve, L, w, t)
                                last = tt(tmp[:, t], tmp[:, t], rstd[:, 0], ALU.add)
                                if w == "bra":
                                    V_(last)
                                else:
                                    last.then_inc(S["mrg"], 1)
                                    wait(dve, "mrg", L, t)
                        elif w in ("q", "cg", "ag"):
                            g_ = (Q["A"] if w == "q" else GT[w[0].upper()])[:, t]
                            wait(dve, "g_tanh", L, t + {"q": 0, "cg": 4, "ag": 8}[w])
                            v.scalar_tensor_tensor(g_, g_, 1.0, ps, ALU.add, ALU.mult).then_inc(evac["V"], 1)
                        elif w == "ca":
                            v.tensor_copy(ca[:, :], ps[0:16]).then_inc(evac["V"], 1)
                        elif w == "cq":
                            v.tensor_single_scalar(Q["C"][:, t], ps, 64.0 ** -0.5, ALU.mult).then_inc(evac["V"], 1)
                        else:
                            dst = {"i": V["A"], "ck": K["C"], "cv": V["C"]}[w]
                            v.tensor_copy(dst[:, t], ps).then_inc(evac["V"], 1)
                    if what == "o" and j == 4:
                        evacuated(dve, L, "adaf", 5)
                        gains(L, 2)
                    place, u = u, OLD[u]
                    if u == 0:
                        wait(dve, "rowsT", L)
                        v.tensor_copy(cbuf[:, :, :], AUX[0][:, 0:128].rearrange("p (j c) -> p j c", j=4))\
                            .then_inc(S["rows_evac"], 1)
                    if u == 4:
                        evacuated(dve, L, "f", 3)
                        V_(v.tensor_single_scalar(x0, z[:, :, :], 0.0, ALU.min))
                        neg_abs(x1, z[:, :, :]).then_inc(S["A_abs"], 1)
                    if u == 6:
                        wait(dve, "A_ln", L)
                        V_(tt(x0, x0, x1, ALU.subtract))
                        own(L)
                        tt(kk[:, :, :], x0, z[:, :, :], ALU.subtract).then_inc(S["A_ls"], 1)
                    if u == 8:
                        wait(dve, "A_k", L)
                        for h in range(H):
                            last = v.tensor_scalar(kk[:, h], kk[:, h], pcol("oml", h), None, ALU.mult)
                            V_(ts(x1[:, h], x0[:, h], pcol("l1m", h), pcol("L1", h), ALU.add, ALU.subtract))
                            V_(ts(z[:, h], x0[:, h], pcol("l1m", h), pcol("L1", h), ALU.add, ALU.max))
                            if h == H - 1:
                                last.then_inc(S["A_kk"], 1)
                        own(L)
                        neg_abs(x1, x1).then_inc(S["A_diff"], 1)
                    if u == 10:
                        wait(dve, "A_ln2", L)
                        tt(z[:, :, :], z[:, :, :], x1, ALU.add).then_inc(S["A_logf"], 1)
                    if u == 11:
                        wait(dve, "A_logf", L)
                        wait(dve, "A_fS", L)
                        for h in range(H):
                            last = v.tensor_tensor_scan(z[:, h, 0:T], ones[:, :], z[:, h, 0:T], 0.0,
                                                        ALU.mult, ALU.add)
                        last.then_inc(S["A_cum"], 1)
                    if u == 15:
                        wait(dve, "C_alpha", L)
                        for jj in range(2):
                            V_(v.tensor_scalar(zc[:, jj, 0:T], AUX[2][:, jj * 256:jj * 256 + 256],
                                               pcol("glab", jj), None, ALU.add))
                            last = v.tensor_scalar(zc[:, jj, T:NT], AUX[3][:, jj * 8:jj * 8 + 8],
                                                   pcol("glab", jj), None, ALU.add)
                        last.then_inc(S["C_z"], 1)
                        wait(dve, "C_z", L)
                        own(L)
                        V_(v.tensor_single_scalar(c0_, zc[:, :, :], 0.0, ALU.min))
                        neg_abs(c1_, zc[:, :, :]).then_inc(S["C_abs"], 1)
                    if u == 17:
                        wait(dve, "C_ln", L)
                        V_(tt(c0_, c0_, c1_, ALU.subtract))
                        own(L)
                        v.tensor_single_scalar(zc[:, :, :], c0_, 1.0 / 16.0, ALU.mult).then_inc(S["C_logf"], 1)
                    if u == 18:
                        wait(dve, "C_logf", L)
                        wait(dve, "C_fS", L)
                        for jj in range(2):
                            last = v.tensor_tensor_scan(zc[:, jj, 0:T], ones[:, :], zc[:, jj, 0:T], 0.0,
                                                        ALU.mult, ALU.add)
                        last.then_inc(S["C_cum"], 1)
                    for n, uu in enumerate((16, 17, 19, 23)):
                        if u == uu:
                            wait(dve, "sT", L, n)
                            w_ = 256 if n == 2 else 512
                            r0 = 32 * (n // 2)
                            v.tensor_copy(sTs[r0:r0 + NB, n % 2, 0:w_], AUX[3][0:NB, 0:w_]).then_inc(S["sTe"], 1)
                    for br in "AC":
                        for li in range(9):
                            if li and u == PE_LV[br][li] - 2:
                                multiply(br, li)
                            if u == PE_LV[br][li] + 1:
                                keep(br, li)
                        if u == (51 if br == "A" else 52):
                            wait(dve, br + "_keexp", L)
                            e = X[br][:, 1, :, 0:T]
                            tt(e, e, K[br][:, :, 0:T], ALU.mult).then_inc(S[br + "_kend"], 1)
                    if u == 26:
                        evacuated(dve, L, "bx", 3)
                        conv_tiles(0, 2)
                    if u == 27:
                        conv_tiles(2, 4)
                        own(L)
                        V_(v.tensor_copy(tail[:, :, 0:11], bx[:, :, T - 3:NT]))
                        own(L)
                        dve.sem_inc(S["conv"], 1)
                    if u == 28:
                        wait(dve, "conv_hi", L)
                        tt(yL[:, 8:12], cv, yH[:, 8:12].bitcast(F), ALU.subtract).then_inc(S["conv_lo"], 1)
                    if u == 31:
                        evacuated(dve, L, "wx", 3)
                        V_(v.scalar_tensor_tensor(bx, bx, 1.0, cv, ALU.add, ALU.mult))
                        for jj in range(4):
                            last = ts(r4[:, jj], r4[:, jj], 1.0, pcol("nsp", jj), ALU.add, ALU.mult)
                        last.then_inc(S["rg_arg"], 1)
                    if u == 33:
                        wait(dve, "rg_tanh", L)
                        own(L)
                        V_(v.scalar_tensor_tensor(cv, r4, 1.0, t4[:, :, :], ALU.add, ALU.mult))
                        own(L)
                        ts(t4[:, :, :], t4[:, :, :], -0.25, 1e-34, ALU.mult, ALU.max).then_inc(S["rg_nt"], 1)
                        V_(v.scalar_tensor_tensor(bx, r4, 1.0, bx, ALU.add, ALU.mult))
                        own(L)
                        V_(v.tensor_single_scalar(r4, cv, 1.0, ALU.add))
                    if u == 35:
                        own(L)
                        wait(dve, "rg_sqrt", L)
                        tt(bx, t4[:, :, :], bx, ALU.mult).then_inc(S["rg_u"], 1)
                    if u == 36:
                        wait(dve, "rg_u", L)
                        for jj in range(4):
                            V_(v.tensor_tensor_scan(cv[:, jj, 0:T], r4[:, jj, 0:T], bx[:, jj, 0:T], 0.0,
                                                    ALU.mult, ALU.add))
                        V_(tt(cv[:, :, T:NT], r4[:, :, T:NT], cbuf[:, :, 24:32], ALU.mult))
                        own(L)
                        V_(tt(cv[:, :, T:NT], cv[:, :, T:NT], bx[:, :, T:NT], ALU.add))
                    if u == 37:
                        own(L)
                        V_(v.tensor_copy(tail[:, :, 11:20], cv[:, :, T - 1:NT]))
                        evacuated(dve, L, "bg", 3)
                        tt(bg, bg, cv, ALU.mult).then_inc(S["yb"], 1)
                    if u == 38:
                        wait(dve, "yb_hi", L)
                        tt(yL[:, 4:8], bg, yH[:, 4:8].bitcast(F), ALU.subtract).then_inc(S["yb_lo"], 1)
                        own(L)
                    if u == 53:
                        wait(dve, "A_kT", L)
                        for t in range(2):
                            last = v.tensor_copy(KTT[:, t], AUX[2 + t][:, :])
                        last.then_inc(S["A_kTe"], 1)
                    if u == 61:
                        wait(dve, "C_kT", L)
                        for t in range(2):
                            last = v.tensor_copy(KTT[:, t, 0:256], AUX[2 + t][:, 0:256])
                        last.then_inc(S["C_kTe"], 1)
                    for i, uu in enumerate((54, 55, 56, 57, 62, 63)):
                        if u == uu:
                            wait(dve, "kv", L, i)
                            dve.wait_ge(st_in[i % 2], L * 64 + st_in_count(i))
                            for b in range(NB):
                                last = v.scalar_tensor_tensor(st[:, i % 2, b], st[:, i % 2, b], fS[:, i, b:b + 1],
                                                              AUX[b // 4][:, (b % 4) * P:(b % 4 + 1) * P],
                                                              ALU.mult, ALU.add)
                            last.then_inc(S["st_new"], 1)
                    for br, uu, y0 in (("A", 59, 0), ("C", 65, 8)):
                        r_ = X["A"][0:H, 1, 0]
                        if place == at(uu, 1):
                            wait(dve, br + "_sq", L)
                            evacuated(dve, L, "ag" if br == "A" else "cg", 3)
                            v.scalar_tensor_tensor(O[br][:, :, :], O[br][:, :, :],
                                                   pcol("hnorm" if br == "A" else "gnorm"), GT[br][:, :, :],
                                                   ALU.mult, ALU.mult).then_inc(S[br + "_w"], 1)
                        if place == at(uu, HEAD["inverse"]):
                            wait(dve, br + "_root", L)
                            v.reciprocal(r_, r_).then_inc(S[br + "_rec"], 1)
                        if place == at(uu, HEAD["scaled"]):
                            wait(dve, br + "_w", L)
                            wait(dve, br + "_spread", L)
                            for h in range(H):
                                last = tt(O[br][:, h], O[br][:, h], AUX[h][:, 0:NT], ALU.mult)
                            last.then_inc(S[br + "_y"], 1)
                        if place == at(uu, HEAD["low"]):
                            wait(dve, br + "_hi", L)
                            tt(yL[:, y0:y0 + 4], O[br][:, :, :], yH[:, y0:y0 + 4].bitcast(F), ALU.subtract)\
                                .then_inc(S[br + "_lo"], 1)
                    if kind == "br" and what == "c":
                        for n in range(2 * j, 2 * j + 2):
                            wait(dve, "m_hi", L, n)
                            tt(yL[:, n], tmp[:, n], yH[:, n].bitcast(F), ALU.subtract).then_inc(S["m_lo"], 1)
                    if u == 69:
                        wait(dve, "tailT", L)
                        v.tensor_copy(crow[0:20, 0:512], AUX[0][0:20, :]).then_inc(S["tail_evac"], 1)
                normed(L, 2)
                low(L, 2)
                gates(L, 2)

            with dve.Fori(0, NL) as L:
                seq[0] = 0
                src = par_all[:, bass.ds(L, 1), :].rearrange("p o n -> p (o n)")
                v.tensor_copy(par[:, :], src).then_inc(S["layer_par"], 1)
                wait(dve, "layer_par", L)
                ada0(L)
                ffn(L, 0)
                mixer(L)
                ffn(L, 1)
                own(L)
                assert seq[0] <= SEQ
                dve.sem_inc(dve_seq, SEQ - seq[0])

            dve.wait_ge(fin_act, 2)
            st_(v.reciprocal(rstd[:, 0], rstd[:, 0]))
            st_(tt(tmp[:, :, :], x[:, :, :], bc(rstd[:, :, :], [P, KT, NT]), ALU.mult))
            fn = par[:, PC["fnorm"]:PC["fnorm"] + 8].rearrange("p (k o) -> p k o", o=1)
            tt(tmp[:, :, :], tmp[:, :, :], bc(fn, [P, KT, NT]), ALU.mult).then_inc(fin_dve, 1)
            dve.wait_ge(fin_pe, 3)
            for half in range(2):
                last = v.tensor_copy(xc[0:NB, 0, half * 512:(half + 1) * 512], BK[4 + half][0:NB, :])
            last.then_inc(fin_dve, 1)


_INS = ['x_prompt', 'x_sample', 'c_prompt', 'c_sample', 'state_hgrn', 'state_conv', 'state_rglru', 'state_gla',
        'w_ada', 'b_ada', 'norm_gain', 'w_ffn_in', 'w_ffn_out', 'w_in', 'hgrn_lb_logits', 'hgrn_norm', 'conv_w',
        'conv_b', 'rg_wa', 'rg_ba', 'rg_wx', 'rg_bx', 'rg_lambda', 'gla_w_alpha', 'gla_b_alpha', 'gla_norm',
        'w_br_a', 'w_br_b', 'w_br_c', 'w_out', 'final_norm']
_OUTS = [(1, T, D), (NB, 1, D), (NL, 1, 4, 128, 128), (NL, NB, 4, 128, 128), (NL, 1, 3, 512), (NL, NB, 3, 512),
         (NL, 1, 512), (NL, NB, 512), (NL, 1, 4, 64, 128), (NL, NB, 4, 64, 128)]


def kernel(**inputs):
    import numpy as _np
    import concourse.bacc as _bacc
    from concourse.bass_utils import run_bass_kernel_spmd as _run

    nc = _bacc.Bacc("TRN2", target_bir_lowering=False, num_devices=1, dynamic_dma_scratch_size=SCRATCH)
    arrays, args = {}, []
    for name in _INS:
        a = _np.ascontiguousarray(inputs[name])
        arrays[f"in_{name}"] = a
        args.append(nc.dram_tensor(f"in_{name}", a.shape, mybir.dt.from_np(a.dtype), kind="ExternalInput").ap())
    for i, shape in enumerate(_OUTS):
        args.append(nc.dram_tensor(f"out_{i}", shape, F, kind="ExternalOutput").ap())
    trunk(nc, *args)
    r = _run(nc, [arrays], core_ids=[0])
    return tuple(r.results[0][f"out_{i}"] for i in range(len(_OUTS)))
```
